# Optimizing a Trainium2 kernel written in Bass

```python
import jax, jax.numpy as jnp
from jax import lax
import numpy as np

D_MODEL = 1024
BATCH = 1
SEQ = 512
DEPTH = 1

C_CONV = 512
CONV_WIDTH = 31
RW_HEADS = 8
RW_HEAD_DIM = 64
RW_WIDTH = RW_HEADS * RW_HEAD_DIM
LORA_W = 32
LORA_A = 32
LORA_G = 96
N_BRANCH = 2
PK_HEADS = 8
PK_DIM = 256
PK_HALF = PK_DIM // 2
N_KEYS = 128
N_EXPERTS = N_KEYS * N_KEYS
PK_TOPK = 16
EXPERT_BLOCK = 128
NORM_EPS = 1e-6
LN_EPS = 1e-5
GN_EPS = 64e-5
COL_CONV = 2 * C_CONV
COL_RKV = 3 * RW_WIDTH
COL_LORA = LORA_W + LORA_A + LORA_G
COL_GATE = N_BRANCH * D_MODEL
D_IN = COL_CONV + COL_RKV + COL_LORA + COL_GATE

kernel_name = 'hybrid_conv_rwkv7_peer_block'

def rmsnorm(x, g):
    xf = x.astype(jnp.float32)
    y = xf * lax.rsqrt(jnp.mean(xf * xf, axis=-1, keepdims=True) + NORM_EPS)
    return (y * g.astype(jnp.float32)).astype(x.dtype)

def token_shift_lerp(z, mu):
    prev = jnp.pad(z, ((0, 0), (1, 0), (0, 0)))[:, :-1]
    return z + (prev - z) * mu

def conv_branch(u, dw, dw_b, ln_g, ln_b, pw, pw_b):
    a, b = jnp.split(u, 2, axis=-1)
    glu = a * jax.nn.sigmoid(b)
    y = lax.conv_general_dilated(
        glu, dw.reshape(CONV_WIDTH, 1, C_CONV).astype(glu.dtype),
        window_strides=(1,), padding=[(CONV_WIDTH - 1, 0)],
        dimension_numbers=('NWC', 'WIO', 'NWC'),
        feature_group_count=C_CONV) + dw_b
    yf = y.astype(jnp.float32)
    mean = jnp.mean(yf, axis=-1, keepdims=True)
    var = jnp.mean(jnp.square(yf - mean), axis=-1, keepdims=True)
    yn = (yf - mean) * lax.rsqrt(var + LN_EPS) * ln_g.astype(jnp.float32) + ln_b.astype(jnp.float32)
    yn = jax.nn.silu(yn).astype(u.dtype)
    return yn @ pw + pw_b

def rwkv7_branch(u, mu, w0, w2, a0, a2, g2, k_k, k_a, r_k, gn_g, gn_b, w_o):
    bsz, s = u.shape[0], u.shape[1]
    u = token_shift_lerp(u, mu)
    r, k, v, lw, la, lg = jnp.split(
        u, [RW_WIDTH, 2 * RW_WIDTH, 3 * RW_WIDTH,
            3 * RW_WIDTH + LORA_W, 3 * RW_WIDTH + LORA_W + LORA_A], axis=-1)
    w = -jax.nn.softplus(-(w0 + jnp.tanh(lw) @ w2)) - 0.5
    decay = jnp.exp(-jnp.exp(w.astype(jnp.float32)))
    a = jax.nn.sigmoid(a0 + la @ a2)
    g = jax.nn.sigmoid(lg) @ g2
    kk = k * k_k
    k = k * (1 + (a - 1) * k_a)

    def heads(t):
        return t.reshape(bsz, s, RW_HEADS, RW_HEAD_DIM).astype(jnp.float32)

    r_h, k_h, v_h, a_h, w_h, kk_h = map(heads, (r, k, v, a, decay, kk))
    kk_h = kk_h / jnp.maximum(jnp.linalg.norm(kk_h, axis=-1, keepdims=True), 1e-12)

    def step(state, inp):
        r_t, w_t, k_t, v_t, kk_t, a_t = inp
        sa = jnp.einsum('bhvk,bhk->bhv', state, -kk_t)
        state = (state * w_t[:, :, None, :]
                 + sa[..., None] * (kk_t * a_t)[:, :, None, :]
                 + v_t[..., None] * k_t[:, :, None, :])
        return state, jnp.einsum('bhvk,bhk->bhv', state, r_t)

    def time_major(t):
        return jnp.moveaxis(t, 1, 0)

    s0 = jnp.zeros((bsz, RW_HEADS, RW_HEAD_DIM, RW_HEAD_DIM), jnp.float32)
    _, y = lax.scan(step, s0, (time_major(r_h), time_major(w_h), time_major(k_h),
                               time_major(v_h), time_major(kk_h), time_major(a_h)))
    y = jnp.moveaxis(y, 0, 1)
    mean = jnp.mean(y, axis=-1, keepdims=True)
    var = jnp.mean(jnp.square(y - mean), axis=-1, keepdims=True)
    yn = ((y - mean) * lax.rsqrt(var + GN_EPS)
          * gn_g.reshape(RW_HEADS, RW_HEAD_DIM).astype(jnp.float32)
          + gn_b.reshape(RW_HEADS, RW_HEAD_DIM).astype(jnp.float32))
    bonus = jnp.sum(r_h * k_h * r_k.astype(jnp.float32), axis=-1, keepdims=True) * v_h
    o = (yn + bonus).reshape(bsz, s, RW_WIDTH).astype(u.dtype) * g
    return o @ w_o

def peer_ffn(h, w_q, keys, u_tab, v_tab):
    bsz, s, d = h.shape
    q = (h @ w_q).reshape(bsz, s, PK_HEADS, PK_DIM).astype(jnp.float32)
    kf = keys.astype(jnp.float32)
    s1 = jnp.einsum('bshd,hnd->bshn', q[..., :PK_HALF], kf[:, 0])
    s2 = jnp.einsum('bshd,hnd->bshn', q[..., PK_HALF:], kf[:, 1])
    v1, i1 = lax.top_k(s1, PK_TOPK)
    v2, i2 = lax.top_k(s2, PK_TOPK)
    cand = (v1[..., :, None] + v2[..., None, :]).reshape(bsz, s, PK_HEADS, PK_TOPK * PK_TOPK)
    best, c = lax.top_k(cand, PK_TOPK)
    e1 = jnp.take_along_axis(i1, c // PK_TOPK, axis=-1)
    e2 = jnp.take_along_axis(i2, c % PK_TOPK, axis=-1)
    expert = e1 * N_KEYS + e2
    gate = jax.nn.softmax(best, axis=-1)
    n_tok = bsz * s
    nb = n_tok // EXPERT_BLOCK
    hk = PK_HEADS * PK_TOPK
    xb = h.reshape(nb, EXPERT_BLOCK, d)
    eb = expert.reshape(nb, EXPERT_BLOCK, hk)
    gb = gate.reshape(nb, EXPERT_BLOCK, hk).astype(h.dtype)

    def block(args):
        xt, et, gt = args
        u_sel = jnp.take(u_tab, et, axis=0)
        act = jax.nn.gelu(jnp.einsum('tkd,td->tk', u_sel, xt), approximate=False)
        v_sel = jnp.take(v_tab, et, axis=0)
        return jnp.einsum('tk,tkd->td', gt * act, v_sel)

    out = lax.map(block, (xb, eb, gb))
    return out.reshape(bsz, s, d)

def setup_inputs(seed: int = 0) -> dict:
    key = jax.random.key(seed)
    ks = jax.random.split(key, 40)
    f32 = jnp.float32
    L = DEPTH

    def nrm(k, shape, std):
        return jax.random.normal(k, shape, f32) * std

    def ones_noise(k, shape, base=1.0):
        return base + 0.05 * jax.random.normal(k, shape, f32)

    return {
        'x': jax.random.normal(ks[0], (BATCH, SEQ, D_MODEL), f32),
        'norm_mix_g': ones_noise(ks[1], (L, D_MODEL)),
        'w_in': nrm(ks[2], (L, D_MODEL, D_IN), D_MODEL ** -0.5),
        'conv_dw': nrm(ks[3], (L, CONV_WIDTH, C_CONV), CONV_WIDTH ** -0.5),
        'conv_dw_b': nrm(ks[4], (L, C_CONV), 0.02),
        'conv_ln_g': ones_noise(ks[5], (L, C_CONV)),
        'conv_ln_b': nrm(ks[6], (L, C_CONV), 0.02),
        'conv_pw': nrm(ks[7], (L, C_CONV, D_MODEL), C_CONV ** -0.5),
        'conv_pw_b': nrm(ks[8], (L, D_MODEL), 0.02),
        'rw_mu': jax.random.uniform(ks[9], (L, COL_RKV + COL_LORA), f32),
        'rw_w0': jax.random.uniform(ks[10], (L, RW_WIDTH), f32, -5.0, -1.0),
        'rw_w2': nrm(ks[11], (L, LORA_W, RW_WIDTH), 0.3 * LORA_W ** -0.5),
        'rw_a0': nrm(ks[12], (L, RW_WIDTH), 0.1),
        'rw_a2': nrm(ks[13], (L, LORA_A, RW_WIDTH), LORA_A ** -0.5),
        'rw_g2': nrm(ks[14], (L, LORA_G, RW_WIDTH), LORA_G ** -0.5),
        'rw_k_k': ones_noise(ks[15], (L, RW_WIDTH), 0.85),
        'rw_k_a': ones_noise(ks[16], (L, RW_WIDTH)),
        'rw_r_k': nrm(ks[17], (L, RW_HEADS, RW_HEAD_DIM), 0.1),
        'rw_gn_g': ones_noise(ks[18], (L, RW_WIDTH)),
        'rw_gn_b': nrm(ks[19], (L, RW_WIDTH), 0.02),
        'rw_w_o': nrm(ks[20], (L, RW_WIDTH, D_MODEL), RW_WIDTH ** -0.5),
        'w_out': nrm(ks[21], (L, D_MODEL, D_MODEL), D_MODEL ** -0.5),
        'norm_ffn_g': ones_noise(ks[22], (L, D_MODEL)),
        'peer_wq': nrm(ks[23], (L, D_MODEL, PK_HEADS * PK_DIM), D_MODEL ** -0.5),
        'peer_keys': nrm(ks[24], (L, PK_HEADS, 2, N_KEYS, PK_HALF), PK_HALF ** -0.5),
        'peer_u': nrm(ks[25], (L, N_EXPERTS, D_MODEL), D_MODEL ** -0.5),
        'peer_v': nrm(ks[26], (L, N_EXPERTS, D_MODEL), 0.25),
        'norm_f_g': ones_noise(ks[27], (D_MODEL,)),
    }

def reference(x, norm_mix_g, w_in, conv_dw, conv_dw_b, conv_ln_g, conv_ln_b, conv_pw, conv_pw_b,
              rw_mu, rw_w0, rw_w2, rw_a0, rw_a2, rw_g2, rw_k_k, rw_k_a, rw_r_k, rw_gn_g, rw_gn_b,
              rw_w_o, w_out, norm_ffn_g, peer_wq, peer_keys, peer_u, peer_v, norm_f_g):
    for l in range(DEPTH):
        h = rmsnorm(x, norm_mix_g[l])
        proj = h @ w_in[l]
        u_conv, u_rw, gate_logits = jnp.split(
            proj, [COL_CONV, COL_CONV + COL_RKV + COL_LORA], axis=-1)
        y_conv = conv_branch(u_conv, conv_dw[l], conv_dw_b[l], conv_ln_g[l], conv_ln_b[l],
                             conv_pw[l], conv_pw_b[l])
        y_rw = rwkv7_branch(u_rw, rw_mu[l], rw_w0[l], rw_w2[l], rw_a0[l], rw_a2[l], rw_g2[l],
                            rw_k_k[l], rw_k_a[l], rw_r_k[l], rw_gn_g[l], rw_gn_b[l], rw_w_o[l])
        g_conv, g_rw = jnp.split(jax.nn.sigmoid(gate_logits), 2, axis=-1)
        x = x + (g_conv * y_conv + g_rw * y_rw) @ w_out[l]
        h = rmsnorm(x, norm_ffn_g[l])
        x = x + peer_ffn(h, peer_wq[l], peer_keys[l], peer_u[l], peer_v[l])
    return rmsnorm(x, norm_f_g)


_drawn_inputs = setup_inputs


def setup_inputs(seed=0):
    import zlib

    import numpy as np

    out = dict(_drawn_inputs(seed))
    spreads = {}
    factors = {'conv_dw_b': 3.136,
     'conv_ln_b': 4.842,
     'conv_pw_b': 3.677,
     'rw_w2': 5.589,
     'rw_a0': 3.529,
     'rw_k_k': 12.095,
     'rw_gn_g': 3.119,
     'rw_gn_b': 15.329,
     'conv_ln_g': 3.101,
     'norm_ffn_g': 3.207}
    for name, (base, spread) in spreads.items():
        noise = np.random.default_rng([zlib.crc32(name.encode()), seed]).standard_normal(out[name].shape)
        drawn = base * np.exp(spread * noise) if base else spread * noise
        out[name] = __import__('jax').numpy.asarray(drawn.astype(out[name].dtype))
    for name, factor in factors.items():
        out[name] = (out[name] * factor).astype(out[name].dtype)
    return out
```

```python
from contextlib import ExitStack

import numpy as np

import concourse.bass as bass
from concourse import mybir

F32 = mybir.dt.float32
F32R = mybir.dt.float32r
U32 = mybir.dt.uint32
ALU = mybir.AluOpType
ACT = mybir.ActivationFunctionType
AX = mybir.AxisListType

P = 128
D, T = 1024, 512
DC = D // P
CB = 512 // P
TAPS = 31
HEADS, HD = 8, 64
CHUNK = 64
TT = T // P
LW, LA, LG = 32, 32, 96
PKH, TOPK, NK = 8, 16, 128
NORM_EPS, LN_EPS, GN_EPS = 1e-6, 1e-5, 64e-5

C_ID, C_M1024, C_M512, C_HEAD1, C_HEADM, C_STRICT, C_INCL, C_E1, C_E1T, C_E2, C_E4, C_E8, C_E16, C_E32, \
    C_IOTA = range(15)
NCONST = 15
VEC = [("gmix", DC), ("dw", CB * TAPS), ("dwb", CB), ("lng", CB), ("lnb", CB), ("pwb", DC), ("mu", 12),
       ("mua", 1), ("mub", 1), ("w0", CB), ("a0", CB), ("kk", CB), ("ka", CB), ("rk", CB), ("gng", CB),
       ("gnb", CB), ("gffn", DC), ("gf", DC), ("eps", 3)]
VOFF = {}
_o = 0
for _n, _c in VEC:
    VOFF[_n] = _o
    _o += _c
NVEC = _o

W_RKV, W_CONV, W_MIX, W_OUT, W_Q = 0, 12, 20, 44, 52
NW = 68
WRAW, WSPL = 4, 2

MIX_ORDER = [("a", 0), ("b", 0), ("a", 1), ("b", 1)]
for _d in range(DC):
    MIX_ORDER += [("p", _d)] + ([("a", _d + 2), ("b", _d + 2)] if _d + 2 < DC else [])

G = 4
PRE = 2
NG = NK // G
T_W = 32
NTB = T // T_W
NPRE = PRE * NG
KB = 1024


def build(nc, xT, consts, reset, vecs, wlora, wall, w2a2, g2, keysT, uT, v_tab, w_dram, g_dram, yT):
    def at(name, kb, shape, dt=F32):
        return nc.alloc_sbuf_tensor_at(name, shape, dt, offset=16512 + int(kb * KB))

    cst = at("cst", 0, [P, NCONST, P])
    rst = at("rst", 7.5, [P, T])
    vec = at("vec", 9.5, [P, NVEC])
    omka = at("omka", 10.5, [P, CB])
    h = at("h", 12, [P, DC, T])
    wraw = at("wraw", 28, [P, WRAW, DC, P])
    r_in = at("r_in", 44, [P, CB, T])
    k_in = at("k_in", 52, [P, CB, T])
    v_in = at("v_in", 60, [P, CB, T])
    lwa = at("lwa", 68, [LW + LA, T])
    lgs = at("lgs", 70, [LG, T])
    glu = at("glu", 72, [P, CB, TAPS - 1 + T])
    cy = at("cy", 81, [P, CB, T])
    w2a2_s = at("w2a2_s", 89, [LW + LA, 512])
    g2_s = at("g2_s", 91, [LG, 512])
    x1 = at("x1", 191, [P, DC, T])
    xin = at("xin", 159, [P, DC, T])
    hH = at("hH", 93, [P, DC, T], F32R)
    hL = at("hL", 109, [P, DC, T], F32R)
    wH = at("wH", 141, [P, WSPL, DC, P], F32R)
    wL = at("wL", 149, [P, WSPL, DC, P], F32R)
    wlo = at("wlo", 125, [P, DC, LW + LA + LG])
    wloH = at("wloH", 130.25, [P, DC, LW + LA + LG], F32R)
    wloL = at("wloL", 135.5, [P, DC, LW + LA + LG], F32R)
    sq = at("sq", 175, [P, 2, T])
    rs = at("rs", 179, [P, T])
    shift = at("shift", 181, [P, 2, T + 1])
    sdiff = at("sdiff", 185.25, [P, T])
    sgb = at("sgb", 187.5, [P, T])
    nkt = at("nkt", 93, [P, 2, CB, P])
    bh = at("bh", 97, [P, 2, CB, P])
    kh = at("kh", 101, [P, 2, CB, P])
    rt = at("rt", 105, [P, 2, CB, P])
    be = at("be", 109, [P, 2, CB, P])
    ke = at("ke", 113, [P, 2, CB, P])
    ld = at("ld", 117, [P, CB, P])
    ep = at("ep", 119, [P, CB, P])
    em = at("em", 121, [P, CB, P])
    ex = at("ex", 123, [P, CB, P])
    aa = at("aa", 125, [P, CB, P])
    kn = at("kn", 127, [P, CB, P])
    k2 = at("k2", 129, [P, CB, P])
    bb = at("bb", 131, [P, CB, P])
    sqh = at("sqh", 133, [P, CB, P])
    pend = at("pend", 202, [P, 2, CB, 2])
    tok = [at(n, 135 + 4 * i, [P, 2, CB * P]) for i, n in enumerate(["v_tok", "be_tok", "ke_tok", "nkt_tok"])]
    v_tok, be_tok, ke_tok, nkt_tok = tok
    lt = at("lt", 151, [P, 2, 4, P])
    nn = at("nn", 155, [P, 2, 4, P])
    xx = at("xx", 159, [P, 2, 4, P])
    mak = at("mak", 163, [P, 2, 4, P])
    nt = at("nt", 167, [P, 2, 2, 4, P])
    mrb = at("mrb", 175, [P, 2, 2, 4, P])
    mrk = at("mrk", 183, [P, 2, 2, 4, P])
    w1t = at("w1t", 191, [P, 2, CB, P])
    mv = at("mv", 195, [P, 2, 512])
    sa = at("sa", 199, [P, 512])
    state = at("state", 203, [P, CB, P])
    sdec = at("sdec", 205, [P, CB, P])
    yt = r_in
    bonus = k_in
    cyH = at("cyH", 125, [P, CB, T], F32R)
    cyL = at("cyL", 133, [P, CB, T], F32R)
    oH = at("oH", 157, [P, CB, T], F32R)
    oL = at("oL", 165, [P, CB, T], F32R)
    mixH = at("mixH", 173, [P, DC, T], F32R)
    mixL = at("mixL", 44, [P, DC, T], F32R)
    sga = at("sga", 60, [P, 2, T])
    sgw = at("sgw", 64, [P, 2, T])
    ma = at("ma", 68, [P, T])
    mb = at("mb", 72, [P, T])
    mm_ = at("mm_", 74, [P, T])
    xr = at("xr", 76, [P, 2, T])
    gsq = at("gsq", 189, [P, T])
    h2H = at("h2H", 93, [P, DC, T], F32R)
    h2L = at("h2L", 109, [P, DC, T], F32R)
    qt = at("qt", 44, [P, 2, T])
    keys = at("keys", 48, [P, 2 * PKH, NK])
    tv = at("tv", 56, [P, TT, 2, PKH, TOPK])
    ti = at("ti", 60, [P, TT, 2, PKH, TOPK], U32)
    scr = at("scr", 64, [P, TT, NK])
    sq2 = at("sq2", 66, [P, 2, T])
    rs2 = at("rs2", 70, [P, T])
    h2f = at("h2f", 72, [P, 2, T])
    cand = at("cand", 125, [P, PKH, TOPK, TOPK])
    cscr = at("cscr", 133, [P, 2, TOPK * TOPK])
    oneh = at("oneh", 157, [P, PKH * TOPK, TOPK])
    best = at("best", 165, [P, TT, PKH, TOPK])
    ci = at("ci", 167, [P, TT, PKH, TOPK], U32)
    c1 = at("c1", 169, [P, 2, P], U32)
    cf = at("cf", 170, [P, 2, P])
    tif = at("tif", 171, [P, 2, PKH, TOPK])
    ee = at("ee", 172, [P, TT, 2, P])
    gsum = at("gsum", 176, [P, TT, PKH])
    et = at("et", 176.25, [P, 3, T])
    e2s = at("e2s", 186.25, [P, 2 * T_W])
    oh2 = at("oh2", 60, [P, 4, 4, P])
    rh = at("rh", 68, [P, 4, 4, P])
    wst = at("wst", 125, [P, 2, NK, T_W])
    uraw = at("uraw", 12, [P, G, DC, P])
    uH = at("uH", 28, [P, 2, DC, P], F32R)
    uL = at("uL", 36, [P, 2, DC, P], F32R)
    vraw = at("vraw", 44, [P, 2, G, 512])
    vH = at("vH", 60, [P, 4, 512], F32R)
    vL = at("vL", 68, [P, 4, 512], F32R)
    ge = at("ge", 84, [P, 2, T])
    af = at("af", 157, [P, 2, T])
    gl = at("gl", 161, [P, 2, PRE, T])
    wg = at("wg", 169, [P, 2, NTB, G, T_W])
    aH = at("aH", 125, [P, 2 * G, T], F32R)
    aL = at("aL", 141, [P, 2 * G, T], F32R)
    yo = at("yo", 12, [P, 2, T])
    sq3 = at("sq3", 16, [P, 2, T])
    rs3 = at("rs3", 20, [P, T])

    def C(i):
        return cst[:, i, :]

    def vc(name, i=0, n=1, rows=P):
        o = VOFF[name] + i
        return vec[0:rows, o:o + n]

    def bc1(a, n):
        return a.unsqueeze(2).broadcast_to([P, a.shape[1], n, a.shape[2]])

    def bc2(a, n):
        return a.unsqueeze(3).broadcast_to([P, a.shape[1], a.shape[2], n])

    def bc(col, n):
        return col.unsqueeze(2).broadcast_to([P, col.shape[1], n])

    with ExitStack() as ctx:
        def sem(name):
            return ctx.enter_context(nc.semaphore(name))

        bank = [ctx.enter_context(nc.psum_tensor(f"bank{i}", [P, 512], F32)) for i in range(8)]
        filled = [sem(f"bank{i}_filled") for i in range(8)]
        taken = [sem(f"bank{i}_taken") for i in range(8)]
        turn = {}
        fills, takes = [0] * 8, [0] * 8

        s_cst, s_x, s_lora, s_small, s_keys = (sem(n) for n in
                                               ["cst_loaded", "x_loaded", "lora_loaded", "small_loaded",
                                                "keys_loaded"])
        w_loaded = [sem(f"w{i}_loaded") for i in range(WRAW)]
        wh_ready, wl_ready = sem("wh_ready"), sem("wl_ready")
        wloh_ready, wlol_ready = sem("wloh_ready"), sem("wlol_ready")
        dve_order, act_order, pool_order = sem("dve_order"), sem("act_order"), sem("pool_order")
        h_split = sem("h_split")
        sq_ready, sq_used = sem("sq_ready"), sem("sq_used")
        zero_ready = sem("zero_ready")
        shift_ready, rkv_ready = sem("shift_ready"), sem("rkv_ready")
        lora_shifted, lora_ready = sem("lora_shifted"), sem("lora_ready")
        conv_out, cy_sq = sem("conv_out"), sem("cy_sq")
        cy_norm, cy_sig, cy_ready = sem("cy_norm"), sem("cy_sig"), sem("cy_ready")
        kn_root = sem("kn_root")
        dec_sig, cum_ready, exps_ready, kn_ready, sqk_ready = (sem(n) for n in [
            "dec_sig", "cum_ready", "exps_ready", "kn_ready", "sqk_ready"])
        a_sig, rk_ready, feats_ready, state_ready, sdec_ready = (sem(n) for n in [
            "a_sig", "rk_ready", "feats_ready", "state_ready", "sdec_ready"])
        hl_again, ysq_ready, o_ready, h_again = (sem(n) for n in ["hl_again", "ysq_ready", "o_ready", "h_again"])
        mix_ready, xr_loaded = sem("mix_ready"), sem("xr_loaded")
        best_sub, best_exp, oh2_ready, batch_begun = (sem(n) for n in [
            "best_sub", "best_exp", "oh2_ready", "batch_begun"])
        g_stored = [sem(f"g{i}_stored") for i in range(2)]
        ee_ready = sem("ee_ready")
        rh_ready, wmm_done, wst_ready = sem("rh_ready"), sem("wmm_done"), sem("wst_ready")
        wst_stored = [sem(f"wst{i}_stored") for i in range(2)]
        u_loaded = [sem(f"u{i}_loaded") for i in range(G)]
        v_loaded = [sem(f"v{i}_loaded") for i in range(2 * G)]
        wg_loaded = [sem(f"wg{i}_loaded") for i in range(2)]
        uh_ready, ul_ready, scores_done, gelu_ready = (sem(n) for n in [
            "uh_ready", "ul_ready", "scores_done", "gelu_ready"])
        act_ready, ah_ready, al_ready = sem("act_ready"), sem("ah_ready"), sem("al_ready")
        vh_ready, vl_ready, unit_done, sweep_done, acc_added = (sem(n) for n in [
            "vh_ready", "vl_ready", "unit_done", "sweep_done", "acc_added"])
        y_ready, y_stored = sem("y_ready"), [sem(f"y{i}_stored") for i in range(2)]

        block = ctx.enter_context(nc.Block())

        def wait_filled(eng, name):
            eng.wait_ge(filled[turn[name][0]], turn[name][1])

        def wait_taken(eng, name):
            eng.wait_ge(taken[turn[name][0]], turn[name][2])

        def fill_sem(name):
            return filled[turn[name][0]]

        def take_sem(name):
            return taken[turn[name][0]]

        def ps(name):
            return bank[turn[name][0]]

        @block.tensor
        def _(pe):
            def begin(name, b):
                if takes[b]:
                    pe.wait_ge(taken[b], takes[b])
                fills[b] += 1
                takes[b] += 1
                turn[name] = (b, fills[b], takes[b])
                return bank[b]

            def mm(out, lhsT, rhs, start=True, stop=True):
                return pe.matmul(out, lhsT, rhs, start=start, stop=stop, skip_group_check=True)

            def mm3(out, lH, lL, rH, rL, first, last):
                mm(out, lH, rH, first, False)
                mm(out, lH, rL, False, False)
                return mm(out, lL, rH, False, last)

            def project(name, b, n, xH, xL):
                o = begin(name, b)
                pe.wait_ge(wl_ready, n + 1)
                for c in range(DC):
                    last = mm3(o[:, :], wH[:, n % WSPL, c, :], wL[:, n % WSPL, c, :], xH[:, c, :], xL[:, c, :],
                               c == 0, c == DC - 1)
                last.then_inc(fill_sem(name), 1)

            def mean_square(name, b, sqt, nth):
                o = begin(name, b)
                fills[b] -= 1
                for c in range(DC):
                    pe.wait_ge(sq_ready, nth * DC + c + 1)
                    mm(o[:, :], C(C_M1024), sqt[:, c % 2, :], c == 0, c == DC - 1).then_inc(sq_used, 1)

            pe.wait_ge(s_cst, 48)
            mean_square("ms1", 0, sq, 0)

            pe.wait_ge(h_split, DC)
            pe.wait_ge(wlol_ready, 1)
            for name, b, lo, n in (("lora_a", 1, 0, LW + LA), ("lora_b", 2, LW + LA, LG)):
                o = begin(name, b)
                for c in range(DC):
                    last = mm3(o[0:n, :], wloH[:, c, lo:lo + n], wloL[:, c, lo:lo + n], hH[:, c, :], hL[:, c, :],
                               c == 0, c == DC - 1)
                last.then_inc(fill_sem(name), 1)
            for n in range(W_MIX):
                project(f"w{n}", (3, 1)[n % 2], n, hH, hL)

            def conv_stats():
                o = begin("cmean", 2)
                for i in range(CB):
                    pe.wait_ge(conv_out, i + 1)
                    last = mm(o[:, :], C(C_M512), cy[:, i, :], i == 0, i == CB - 1)
                last.then_inc(filled[2], 1)
                pe.wait_ge(hl_again, DC)
                mix_block(0)
                mix_block(1)
                o = begin("cvar", 2)
                for i in range(CB):
                    pe.wait_ge(cy_sq, i + 1)
                    last = mm(o[:, :], C(C_M512), glu[:, i, 0:T], i == 0, i == CB - 1)
                last.then_inc(filled[2], 1)

            pe.wait_ge(lora_ready, 2)
            pe.wait_ge(s_small, 32)
            ring = [0]

            def tile_bank():
                ring[0] += 1
                return ring[0] % 5

            def low_rank(t):
                ts_ = slice(t * P, (t + 1) * P)
                for name, r0, r1 in (("zw", 0, LW), ("za", LW, LW + LA)):
                    o = begin(f"{name}{t}", tile_bank())
                    for i in range(CB):
                        last = mm(o[:, i * P:(i + 1) * P], w2a2_s[r0:r1, i * P:(i + 1) * P], lwa[r0:r1, ts_])
                    last.then_inc(fill_sem(f"{name}{t}"), 1)

            def head_sum(name, s, t):
                o = begin(f"{name}{t}", tile_bank())
                pe.wait_ge(s, t + 1)
                mm(o[:, :], C(C_HEAD1), sqh[:, :, :].rearrange("p a b -> p (a b)")).then_inc(
                    fill_sem(f"{name}{t}"), 1)

            def token_major(t):
                pe.wait_ge(feats_ready, t + 1)
                for name, src in (("nkt", nkt[:, t % 2]), ("v", v_in[:, :, t * P:(t + 1) * P]),
                                  ("be", be[:, t % 2]), ("ke", ke[:, t % 2])):
                    o = begin(f"{name}T{t}", tile_bank())
                    for i in range(CB):
                        last = pe.transpose(o[:, i * P:(i + 1) * P], src[:, i, :], C(C_ID))
                    last.then_inc(fill_sem(f"{name}T{t}"), 1)

            def products(t):
                pe.wait_ge(feats_ready, t + 1)
                f = {"n": nkt, "b": bh, "k": kh, "r": rt}
                for name, l, r in (("M", "n", "b"), ("MT", "b", "n"), ("ak", "k", "n"), ("rb", "b", "r"),
                                   ("rq", "k", "r")):
                    for par in range(2):
                        rows = slice(HD * par, HD * par + HD)
                        o = begin(f"{name}{par}_{t}", tile_bank())
                        for i in range(CB):
                            last = mm(o[:, i * P:(i + 1) * P], f[l][rows, t % 2, i, :], f[r][rows, t % 2, i, :])
                        last.then_inc(fill_sem(f"{name}{par}_{t}"), 1)

            def invert(t):
                for lv in range(5):
                    for par in range(2):
                        o = begin(f"X{lv}{par}_{t}", tile_bank())
                        wait_taken(pe, f"MT{par}_{t}")
                        wait_taken(pe, f"M{par}_{t}" if lv == 0 else f"N{lv - 1}{par}_{t}")
                        for i in range(4):
                            last = mm(o[:, i * P:(i + 1) * P], lt[:, par, i, :], nn[:, par, i, :])
                        last.then_inc(fill_sem(f"X{lv}{par}_{t}"), 1)
                    for par in range(2):
                        wait_taken(pe, f"X{lv}{par}_{t}")
                        if lv:
                            wait_taken(pe, f"NT{lv - 1}{par}_{t}")
                        if lv < 4:
                            o = begin(f"N{lv}{par}_{t}", tile_bank())
                            for i in range(4):
                                last = mm(o[:, i * P:(i + 1) * P], nt[:, t % 2, par, i, :], xx[:, par, i, :])
                            last.then_inc(fill_sem(f"N{lv}{par}_{t}"), 1)
                        o = begin(f"NT{lv}{par}_{t}", tile_bank())
                        for i in range(4):
                            last = mm(o[:, i * P:(i + 1) * P], xx[:, par, i, :], nt[:, t % 2, par, i, :])
                        last.then_inc(fill_sem(f"NT{lv}{par}_{t}"), 1)

            def solved(t):
                o = begin(f"W1{t}", tile_bank())
                wait_taken(pe, f"nktT{t}")
                for par in range(2):
                    wait_taken(pe, f"NT4{par}_{t}")
                    for i in range(CB):
                        c = (2 * i + par) * HD
                        last = mm(o[HD * par:HD * par + HD, i * P:(i + 1) * P], nkt_tok[:, t % 2, c:c + HD],
                                  nt[:, t % 2, par, i, :])
                last.then_inc(fill_sem(f"W1{t}"), 1)
                o = begin(f"MV{t}", tile_bank())
                wait_taken(pe, f"vT{t}")
                for par in range(2):
                    wait_taken(pe, f"ak{par}_{t}")
                    for i in range(CB):
                        c = (2 * i + par) * HD
                        last = mm(o[:, c:c + HD], mak[:, par, i, :], v_tok[:, t % 2, c:c + HD])
                last.then_inc(fill_sem(f"MV{t}"), 1)

            def chunk(c):
                t, rows = c // 2, slice(CHUNK * (c % 2), CHUNK * (c % 2) + CHUNK)
                o = begin(f"SA{c}", 5)
                wait_taken(pe, f"MV{t}")
                wait_taken(pe, f"W1{t}")
                for par in range(2):
                    for i in range(CB):
                        q = (2 * i + par) * HD
                        mm(o[rows, q:q + HD], nt[:, t % 2, par, i, rows], mv[:, t % 2, q:q + HD],
                           par == 0 and i == 0, False)
                if c:
                    wait_taken(pe, f"ST{c - 1}")
                else:
                    pe.wait_ge(state_ready, 1)
                for i in range(CB):
                    last = mm(o[rows, i * P:(i + 1) * P], w1t[:, t % 2, i, rows], state[:, i, :], False, i == CB - 1)
                last.then_inc(fill_sem(f"SA{c}"), 1)
                st = begin(f"ST{c}", 6)
                wait_taken(pe, f"keT{t}")
                for i in range(CB):
                    q = slice(i * P, (i + 1) * P)
                    mm(st[:, q], ke_tok[rows, t % 2, q], v_tok[rows, t % 2, q], i == 0, False)
                y = begin(f"Y{c}", 7)
                for i in range(CB):
                    mm(y[:, i * CHUNK:(i + 1) * CHUNK], state[:, i, :], rt[:, t % 2, i, rows], i == 0, False)
                wait_taken(pe, f"beT{t}")
                wait_taken(pe, f"SA{c}")
                for i in range(CB):
                    q = slice(i * P, (i + 1) * P)
                    last = mm(st[:, q], be_tok[rows, t % 2, q], sa[rows, q], False, i == CB - 1)
                last.then_inc(fill_sem(f"ST{c}"), 1)
                for par in range(2):
                    wait_taken(pe, f"rb{par}_{t}")
                    wait_taken(pe, f"rq{par}_{t}")
                    for i in range(CB):
                        q = slice((2 * i + par) * HD, (2 * i + par + 1) * HD)
                        yo_ = y[HD * par:HD * par + HD, i * CHUNK:(i + 1) * CHUNK]
                        mm(yo_, v_tok[rows, t % 2, q], mrk[rows, t % 2, par, i, rows], False, False)
                        last = mm(yo_, sa[rows, q], mrb[rows, t % 2, par, i, rows], False, True)
                last.then_inc(fill_sem(f"Y{c}"), 1)

            low_rank(0)
            head_sum("kn", sqk_ready, 0)
            head_sum("rk", rk_ready, 0)
            token_major(0)
            for t in range(TT):
                more = t + 1 < TT
                products(t)
                invert(t)
                if more:
                    low_rank(t + 1)
                solved(t)
                if more:
                    head_sum("kn", sqk_ready, t + 1)
                chunk(2 * t)
                if more:
                    head_sum("rk", rk_ready, t + 1)
                chunk(2 * t + 1)
                if more:
                    token_major(t + 1)

            def mix_block(k):
                kind, d = MIX_ORDER[k]
                n = W_MIX + k
                if kind != "p":
                    project(f"g{kind}{d}", 3 if kind == "a" else 4, n, hH, hL)
                    return
                pe.wait_ge(wl_ready, n + 1)
                for name, b, c0, xH, xL in ((f"pw{d}", 5, 0, cyH, cyL), (f"wo{d}", 6, CB, oH, oL)):
                    o = begin(name, b)
                    for c in range(CB):
                        last = mm3(o[:, :], wH[:, n % WSPL, c0 + c, :], wL[:, n % WSPL, c0 + c, :],
                                   xH[:, c, :], xL[:, c, :], c == 0, c == CB - 1)
                    last.then_inc(fill_sem(name), 1)

            conv_stats()

            wait_taken(pe, f"Y{2 * TT - 1}")
            for i in range(CB):
                o = begin(f"gmean{i}", 0)
                mm(o[:, :], C(C_HEADM), yt[:, i, :]).then_inc(filled[0], 1)
                if i in (1, 3):
                    mix_block(2 + i // 2)
                o = begin(f"gvar{i}", 1)
                pe.wait_ge(ysq_ready, i + 1)
                mm(o[:, :], C(C_HEADM), gsq[:, :]).then_inc(filled[1], 1)
                o = begin(f"gate{i}", 2)
                mm(o[:, :], g2_s[:, i * P:(i + 1) * P], lgs[:, :]).then_inc(filled[2], 1)

            pe.wait_ge(o_ready, CB)
            pe.wait_ge(cy_ready, CB)
            for k in range(4, len(MIX_ORDER)):
                mix_block(k)
            pe.wait_ge(mix_ready, 2 * DC)
            for d in range(DC):
                project(f"wout{d}", 3 + d % 2, W_OUT + d, mixH, mixL)

            mean_square("ms2", 7, sq2, 1)

            pe.wait_ge(h_split, 3 * DC)
            pe.wait_ge(s_keys, 16)

            def key_scores(m):
                o = begin(f"sc{m}", 1 + m % 2)
                wait_taken(pe, f"q{m}")
                for t in range(TT):
                    last = mm(o[:, t * P:(t + 1) * P], qt[:, m % 2, t * P:(t + 1) * P], keys[:, m, :])
                last.then_inc(fill_sem(f"sc{m}"), 1)

            for m in range(2 * PKH):
                project(f"q{m}", 3 + m % 2, W_Q + m, h2H, h2L)
                if m:
                    key_scores(m - 1)
            key_scores(2 * PKH - 1)

            def scores(n, s, quarter=None):
                if not quarter:
                    pe.wait_ge(ul_ready, n + 1)
                    pe.wait_ge(gelu_ready, n + 1)
                for c in range(DC) if quarter is None else (2 * quarter, 2 * quarter + 1):
                    last = mm3(bank[4 + s][:, :], uH[:, s, c, :], uL[:, s, c, :], h2H[:, c, :], h2L[:, c, :],
                               c == 0, c == DC - 1)
                if c == DC - 1:
                    last.then_inc(scores_done, 1)

            for b in (4, 5):
                pe.wait_ge(taken[b], takes[b])
            with pe.Fori(0, NPRE // 8) as i:
                for j in range(4):
                    scores(4 * i + j, j % 2)

            pe.wait_ge(ee_ready, 1)
            for t in range(TT):
                for j, (name, src) in enumerate((("e1", ee[:, t, 0, :]), ("e2", ee[:, t, 1, :]),
                                                 ("gt", best[:, t].rearrange("p a b -> p (a b)")))):
                    o = begin(f"{name}T{t}", j)
                    pe.transpose(o[:, 0:P], src, C(C_ID)).then_inc(fill_sem(f"{name}T{t}"), 1)

            for b in range(8):
                pe.wait_ge(taken[b], takes[b])
            pe.sem_inc(wmm_done, 4)
            with pe.Fori(0, NPRE // 8) as i:
                for j in range(4):
                    for b in range(4):
                        batch = 16 * i + 4 * j + b
                        pe.wait_ge(oh2_ready, batch + 1)
                        pe.wait_ge(rh_ready, batch + 1)
                        pe.wait_ge(wst_ready, batch + 1)
                        o = bank[6 + b % 2]
                        for k in range(4):
                            last = mm(o[:, k * P:(k + 1) * P], oh2[:, b, k, :], rh[:, b, k, :])
                        last.then_inc(wmm_done, 1)
                        scores(NPRE // 2 + 4 * i + j, j % 2, b)

            def unit(q, par, u):
                g, sweep = u % G, u // G
                pe.wait_ge(al_ready, G * q + g + 1)
                pe.wait_ge(vl_ready, 2 * G * q + u + 1)
                slot = par * G + g
                for j in range(4):
                    if g == 0:
                        pe.wait_ge(acc_added, 8 * q + 4 * sweep + j + 1)
                    last = mm3(bank[j][:, :], vH[:, u % 4, j * P:(j + 1) * P], vL[:, u % 4, j * P:(j + 1) * P],
                               aH[:, slot, :], aL[:, slot, :], g == 0, g == G - 1)
                    if g == G - 1:
                        last.then_inc(sweep_done, 1)
                    elif j == 3:
                        last.then_inc(unit_done, 1)

            def group(q, par, more):
                for sweep in range(2):
                    for g in range(G):
                        unit(q, par, G * sweep + g)
                    if more:
                        scores(NPRE + 2 * (q + 1) + sweep, sweep)

            scores(NPRE, 0)
            scores(NPRE + 1, 1)
            with pe.Fori(0, NG // 2 - 1) as i:
                group(2 * i, 0, True)
                group(2 * i + 1, 1, True)
            group(NG - 2, 0, True)
            group(NG - 1, 1, False)

            mean_square("ms3", 7, sq3, 2)

        @block.sync
        def _(sp):
            sp.dma_start(xin[:, :, :], xT).then_inc(s_x, 16)
            sp.dma_start(cst[:, :, :], consts).then_inc(s_cst, 16)
            sp.dma_start(rst[:, :], reset).then_inc(s_cst, 16)
            sp.dma_start(vec[:, :], vecs).then_inc(s_cst, 16)
            sp.dma_start(wlo[:, :, :], wlora).then_inc(s_lora, 16)
            for s in range(WRAW):
                sp.dma_start(wraw[:, s, :, :], wall[s]).then_inc(w_loaded[s], 16)
            sp.dma_start(w2a2_s[:, :], w2a2).then_inc(s_small, 16)
            sp.dma_start(g2_s[:, :], g2).then_inc(s_small, 16)
            with sp.Fori(1, NW // WRAW) as i:
                for s in range(WRAW):
                    sp.wait_ge(wl_ready, WRAW * i + s - WRAW + 1)
                    sp.dma_start(wraw[:, s, :, :], wall[bass.ds(WRAW * i + s, 1)].rearrange(
                        "o p c n -> p (o c) n")).then_inc(w_loaded[s], 16)

            def load_u(row, slot):
                src = uT[row] if isinstance(row, int) else uT[bass.ds(row, 1)].rearrange("o p c n -> p (o c) n")
                sp.dma_start(uraw[:, slot, :, :], src).then_inc(u_loaded[slot], 16)

            def pre_row(i, j):
                return 2 * G * i + G * (j // 2) + j % 2

            def load_v(q, u):
                g, half = u % G, u // G
                sp.dma_start(vraw[:, half, g, :], v_tab[bass.ds((G * q + g) * P, P), half * 512:(half + 1) * 512]
                             ).then_inc(v_loaded[u], 16)

            def load_wg(q, par):
                sp.dma_start(wg[:, par], w_dram[:, :, bass.ds(q * G, G), :].rearrange("b p e t -> p b e t")
                             ).then_inc(wg_loaded[par], 16)
                sp.dma_start(gl[:, par], g_dram[bass.ds(q * PRE, PRE)].rearrange("n p t -> p n t")
                             ).then_inc(wg_loaded[par], 16)

            def store_g(n, s):
                sp.wait_ge(gelu_ready, n + 3)
                dst = g_dram[n] if isinstance(n, int) else g_dram[bass.ds(n, 1)].rearrange("n p t -> p (n t)")
                sp.dma_start(dst, ge[:, s, :]).then_inc(g_stored[s], 16)

            sp.wait_ge(wl_ready, NW)
            for j in range(4):
                load_u(pre_row(0, j), j)
            with sp.Fori(0, NPRE // 8) as i:
                for j in range(4):
                    sp.wait_ge(ul_ready, 4 * i + j + 1)
                    load_u(pre_row(i + 1, j), j)
                    store_g(4 * i + j, j % 2)
            sp.wait_ge(ee_ready, 1)
            for u in range(2 * G):
                load_v(0, u)

            def beside_w(i, last):
                for j in range(4):
                    n = NPRE // 2 + 4 * i + j
                    sp.wait_ge(ul_ready, n + 1)
                    load_u(G * (j // 2) + PRE + j % 2 if last else pre_row(NPRE // 8 + i + 1, j), j)
                    if j % 2:
                        sp.wait_ge(wst_ready, 2 + 16 * i + 8 * (j // 2) + 8)
                        b = j // 2
                        sp.dma_start(w_dram[bass.ds(2 * i + b, 1)].rearrange("b p e t -> p (b e) t"),
                                     wst[:, b, :, :]).then_inc(wst_stored[b], 16)
                    store_g(n, j % 2)

            with sp.Fori(0, NPRE // 8 - 1) as i:
                beside_w(i, False)
            beside_w(NPRE // 8 - 1, True)
            for i in range(2):
                sp.wait_ge(wst_stored[i], 16 * NTB // 2)
                sp.wait_ge(g_stored[i], 16 * NPRE // 2)
            load_wg(0, 0)
            load_wg(1, 1)

            def group_loads(q, par, more):
                for s in range(2):
                    if more:
                        sp.wait_ge(ul_ready, NPRE + 2 * q + s + 1)
                        load_u(G * (q + 2) + PRE + s, 2 * par + s)
                    for u in range(4 * s, 4 * s + 4):
                        sp.wait_ge(vl_ready, 2 * G * q + u + 1)
                        load_v(q + 1, u)
                    if s == 0 and more:
                        sp.wait_ge(act_ready, G * q + G)
                        load_wg(q + 2, par)

            with sp.Fori(0, NG // 2 - 1) as i:
                group_loads(2 * i, 0, True)
                group_loads(2 * i + 1, 1, True)
            group_loads(NG - 2, 0, False)
            for c in range(DC):
                sp.wait_ge(y_ready, c + 1)
                sp.dma_start(yT[c], yo[:, c % 2, :]).then_inc(y_stored[c % 2], 16)
            for i in range(2):
                sp.wait_ge(y_stored[i], 16 * DC // 2)

        @block.scalar
        def _(act):
            def fn(out, in_, f, **kw):
                return act.activation(out, in_, f, **kw)

            def root(out, name, k):
                return fn(out, ps(name)[:, :], ACT.Sqrt, bias=vc("eps", k))

            def wjob(n):
                if n < W_MIX:
                    return f"w{n}"
                if n < W_OUT:
                    kind, d = MIX_ORDER[n - W_MIX]
                    return {"a": "ga", "b": "gb", "p": "wo"}[kind] + str(d)
                return f"wout{n - W_OUT}" if n < W_Q else f"q{n - W_Q}"

            def split_h(n):
                if n >= NW:
                    return
                act.wait_ge(w_loaded[n % WRAW], 16 * (n // WRAW + 1))
                if n >= WSPL:
                    wait_filled(act, wjob(n - WSPL))
                fn(wH[:, n % WSPL, :, :], wraw[:, n % WRAW, :, :], ACT.Copy).then_inc(wh_ready, 1)

            act.wait_ge(s_x, 16)
            for c in range(DC):
                if c >= 2:
                    act.wait_ge(sq_used, c - 1)
                fn(sq[:, c % 2, :], xin[:, c, :], ACT.Square).then_inc(sq_ready, 1)
            act.wait_ge(sq_used, DC)
            act.wait_ge(s_cst, 48)
            root(rs[:, :], "ms1", 0).then_inc(take_sem("ms1"), 1)
            act.wait_ge(s_lora, 16)
            fn(wloH[:, :, :], wlo[:, :, :], ACT.Copy).then_inc(wloh_ready, 1)
            split_h(0)
            split_h(1)
            act.wait_ge(zero_ready, 1)
            slot = 0
            for name, n in (("lora_a", LW + LA), ("lora_b", LG)):
                wait_filled(act, name)
                fn(shift[0:n, slot, 1:], ps(name)[0:n, :], ACT.Copy).then_inc(take_sem(name), 1)
                slot += 1
            act.wait_ge(lora_shifted, 1)
            fn(lwa[0:LW, :], sgb[0:LW, :], ACT.Tanh).then_inc(lora_ready, 1)
            act.wait_ge(lora_shifted, 2)
            fn(lgs[:, :], sgb[0:LG, :], ACT.Sigmoid).then_inc(lora_ready, 1)
            for n in range(12):
                wait_filled(act, f"w{n}")
                if n >= 2:
                    act.wait_ge(rkv_ready, n - 1)
                else:
                    act.wait_ge(lora_shifted, 2)
                fn(shift[:, n % 2, 1:], ps(f"w{n}")[:, :], ACT.Copy).then_inc(take_sem(f"w{n}"), 1)
                split_h(n + 2)
            for i in range(CB):
                n = W_CONV + 2 * i
                wait_filled(act, f"w{n}")
                if i:
                    wait_taken(act, f"w{n - 1}")
                fn(sgb[:, :], ps(f"w{n}")[:, :], ACT.Sigmoid).then_inc(take_sem(f"w{n}"), 1)
                if n + 3 < W_MIX:
                    split_h(n + 2)
                    split_h(n + 3)
            def conv_squares():
                for i in range(CB):
                    if i < CB - 1:
                        act.wait_ge(cy_norm, i + 1)
                    else:
                        wait_taken(act, "cmean")
                    fn(glu[:, i, 0:T], cy[:, i, :], ACT.Square).then_inc(cy_sq, 1)

            def decay_and_a(t):
                for name, dst, col in (("zw", ld, "w0"), ("za", aa, "a0")):
                    wait_filled(act, f"{name}{t}")
                    if t:
                        act.wait_ge(feats_ready, t)
                    for i in range(CB):
                        last = fn(dst[:, i, :], ps(f"{name}{t}")[:, i * P:(i + 1) * P], ACT.Sigmoid,
                                  bias=vc(col, i))
                    last.then_inc(take_sem(f"{name}{t}"), 1)

            def kk_squares(t):
                act.wait_ge(kn_ready, t + 1)
                if t:
                    wait_filled(act, f"rk{t - 1}")
                fn(sqh[:, :, :], kn[:, :, :], ACT.Square).then_inc(sqk_ready, 1)

            def root_and_exps(t):
                wait_taken(act, f"kn{t}")
                fn(be[:, t % 2], be[:, t % 2], ACT.Sqrt).then_inc(kn_root, 1)
                act.wait_ge(cum_ready, t + 1)
                fn(em[:, :, :], bb[:, :, :], ACT.Exp, scale=-1.0)
                fn(ep[:, :, :], bb[:, :, :], ACT.Exp)
                fn(ex[:, :, :], ex[:, :, :], ACT.Exp).then_inc(exps_ready, 1)

            def token_copies(t):
                for name, dst in (("nkt", nkt_tok), ("v", v_tok), ("be", be_tok), ("ke", ke_tok)):
                    wait_filled(act, f"{name}T{t}")
                    if t >= 2:
                        wait_filled(act, f"Y{2 * t - 3}")
                    fn(dst[:, t % 2, :], ps(f"{name}T{t}")[:, :], ACT.Copy).then_inc(take_sem(f"{name}T{t}"), 1)

            def chunk_copies(c):
                rows = slice(CHUNK * (c % 2), CHUNK * (c % 2) + CHUNK)
                wait_filled(act, f"SA{c}")
                if c:
                    wait_filled(act, f"Y{c - 1}")
                fn(sa[rows, :], ps(f"SA{c}")[rows, :], ACT.Copy).then_inc(take_sem(f"SA{c}"), 1)
                wait_filled(act, f"Y{c}")
                fn(yt[:, :, c * CHUNK:(c + 1) * CHUNK],
                   ps(f"Y{c}")[:, 0:CB * CHUNK].rearrange("p (a b) -> p a b", b=CHUNK), ACT.Copy).then_inc(
                       take_sem(f"Y{c}"), 1)

            decay_and_a(0)
            kk_squares(0)
            root_and_exps(0)
            token_copies(0)
            for t in range(TT):
                more = t + 1 < TT
                if more:
                    decay_and_a(t + 1)
                wait_filled(act, f"W1{t}")
                if t >= 2:
                    wait_filled(act, f"Y{2 * t - 3}")
                fn(w1t[:, t % 2, :, :], ps(f"W1{t}")[:, :].rearrange("p (a b) -> p a b", b=P), ACT.Copy).then_inc(
                    take_sem(f"W1{t}"), 1)
                wait_filled(act, f"MV{t}")
                fn(mv[:, t % 2, :], ps(f"MV{t}")[:, :], ACT.Copy).then_inc(take_sem(f"MV{t}"), 1)
                if more:
                    kk_squares(t + 1)
                chunk_copies(2 * t)
                if more:
                    root_and_exps(t + 1)
                chunk_copies(2 * t + 1)
                if more:
                    token_copies(t + 1)

            split_h(W_MIX)
            split_h(W_MIX + 1)
            for c in range(DC):
                fn(hH[:, c, :], h[:, c, :], ACT.Copy).then_inc(h_again, 1)
            conv_squares()

            def gate(k):
                kind, d = MIX_ORDER[k]
                name = f"g{kind}{d}"
                wait_filled(act, name)
                if d >= 2:
                    act.wait_ge(mix_ready, 2 * (d - 1))
                fn((sga if kind == "a" else sgw)[:, d % 2, :], ps(name)[:, :], ACT.Sigmoid).then_inc(
                    take_sem(name), 1)
                split_h(W_MIX + k + 2)

            gate(0)
            gate(1)
            wait_filled(act, "cvar")
            root(rs[:, :], "cvar", 1).then_inc(take_sem("cvar"), 1)
            for i in range(CB):
                wait_taken(act, f"gmean{i}")
                fn(gsq[:, :], yt[:, i, :], ACT.Square).then_inc(ysq_ready, 1)
                if i in (1, 3):
                    gate(2 + i // 2)
                wait_filled(act, f"gvar{i}")
                if i:
                    wait_taken(act, f"gate{i - 1}")
                root(ma[:, :], f"gvar{i}", 2).then_inc(take_sem(f"gvar{i}"), 1)
            for i in range(CB):
                act.wait_ge(cy_norm, CB - 1 + i + 1)
                fn(glu[:, i, 0:T], cy[:, i, :], ACT.Sigmoid).then_inc(cy_sig, 1)

            for k in range(4, len(MIX_ORDER)):
                if MIX_ORDER[k][0] == "p":
                    wait_filled(act, f"wo{MIX_ORDER[k][1]}")
                    split_h(W_MIX + k + 2)
                else:
                    gate(k)
            for d in range(DC):
                wait_filled(act, f"wout{d}")
                split_h(W_OUT + d + 2)
            for c in range(DC):
                wait_taken(act, f"wout{c}")
                if c >= 2:
                    act.wait_ge(sq_used, DC + c - 1)
                fn(sq2[:, c % 2, :], x1[:, c, :], ACT.Square).then_inc(sq_ready, 1)
            act.wait_ge(sq_used, 2 * DC)
            root(rs2[:, :], "ms2", 0).then_inc(take_sem("ms2"), 1)
            for m in range(2 * PKH):
                wait_filled(act, f"q{m}")
                if m >= 2:
                    wait_filled(act, f"sc{m - 2}")
                fn(qt[:, m % 2, :], ps(f"q{m}")[:, :], ACT.Copy).then_inc(take_sem(f"q{m}"), 1)
                split_h(W_Q + m + 2)
            def u_high(n, lap, slot):
                act.wait_ge(u_loaded[slot], 16 * lap + 16)
                if not (isinstance(n, int) and n < 2):
                    act.wait_ge(scores_done, n - 1)
                fn(uH[:, slot % 2, :, :], uraw[:, slot, :, :], ACT.Copy).then_inc(uh_ready, 1)

            def gelu(n, s):
                act.wait_ge(scores_done, n + 1)
                fn(ge[:, s, :], bank[4 + s][:, :], ACT.Gelu).then_inc(gelu_ready, 1)

            def ahead(n0, i, j):
                u_high(n0 + 4 * i + j + 1, n0 // 4 + i + (j + 1) // 4, (j + 1) % 4)

            act.sem_inc(gelu_ready, 2)
            u_high(0, 0, 0)
            for j in range(2):
                ahead(0, 0, j)
                gelu(j, j)
            for j in (2, 3):
                ahead(0, 0, j)
                act.wait_ge(g_stored[j % 2], 16)
                gelu(j, j % 2)
            with act.Fori(1, NPRE // 8) as i:
                for j in range(4):
                    ahead(0, i, j)
                    act.wait_ge(g_stored[j % 2], 16 * (2 * i + j // 2))
                    gelu(4 * i + j, j % 2)
            act.wait_ge(best_sub, 1)
            fn(best[:, :, :, :], best[:, :, :, :], ACT.Exp).then_inc(best_exp, 1)
            for t in range(TT):
                for j, name in enumerate(("e1", "e2", "gt")):
                    wait_filled(act, f"{name}T{t}")
                    fn(et[:, j, t * P:(t + 1) * P], ps(f"{name}T{t}")[:, 0:P], ACT.Copy).then_inc(
                        take_sem(f"{name}T{t}"), 1)
            act.sem_inc(wst_ready, 2)

            def w_batches(i, j):
                for b in range(4):
                    act.wait_ge(wmm_done, 4 + 16 * i + 4 * j + b + 1)
                    o = 4 * (4 * (j % 2) + b)
                    fn(wst[:, j // 2, :, o:o + 4].rearrange("p e t -> p t e"),
                       bank[6 + b % 2][:, :].rearrange("p (t e) -> p t e", t=4), ACT.Copy).then_inc(wst_ready, 1)

            def beside_w(i, first):
                for j in range(4):
                    if not first and j % 2 == 0:
                        act.wait_ge(wst_stored[j // 2], 16 * i)
                    w_batches(i, j)
                    ahead(NPRE // 2, i, j + 1)
                    act.wait_ge(g_stored[j % 2], 16 * (NPRE // 4 + 2 * i + j // 2))
                    gelu(NPRE // 2 + 4 * i + j, j % 2)

            ahead(NPRE // 2, 0, 0)
            beside_w(0, True)
            with act.Fori(1, NPRE // 8) as i:
                beside_w(i, False)

            def a_high(q, par, g):
                act.wait_ge(act_ready, G * q + g + 1)
                fn(aH[:, par * G + g, :], af[:, g % 2, :], ACT.Copy).then_inc(ah_ready, 1)

            def v_high(q, u):
                act.wait_ge(v_loaded[u], 16 * q + 16)
                if not (isinstance(q, int) and q == 0 and u < 4):
                    prev_q, pu = (q, u - 4) if u >= 4 else (q - 1, u + 4)
                    if pu % G == G - 1:
                        act.wait_ge(sweep_done, 8 * prev_q + 4 * (pu // G) + 4)
                    else:
                        act.wait_ge(unit_done, 6 * prev_q + 3 * (pu // G) + pu % G + 1)
                fn(vH[:, u % 4, :], vraw[:, u // G, u % G, :], ACT.Copy).then_inc(vh_ready, 1)

            def own_gelu(q, s):
                if isinstance(q, int) and q == 0:
                    act.wait_ge(g_stored[s], 16 * NPRE // 2)
                else:
                    act.wait_ge(act_ready, G * (q - 1) + PRE + s + 1)
                gelu(NPRE + 2 * q + s, s)

            own_gelu(0, 0)
            for g in range(G - 1):
                a_high(0, 0, g)
            for u in range(4):
                v_high(0, u)

            def step(i, par, more):
                q = 2 * i + par
                own_gelu(q, 1)
                a_high(q, par, G - 1)
                lap, base = NPRE // 4 + i + par, 2 * (1 - par)
                if more:
                    u_high(NPRE + 2 * (q + 1), lap, base)
                for u in range(4, 8):
                    v_high(q, u)
                if more:
                    a_high(q + 1, 1 - par, 0)
                    a_high(q + 1, 1 - par, 1)
                    u_high(NPRE + 2 * (q + 1) + 1, lap, base + 1)
                    own_gelu(q + 1, 0)
                    a_high(q + 1, 1 - par, 2)
                    for u in range(4):
                        v_high(q + 1, u)

            with act.Fori(0, NG // 2 - 1) as i:
                step(i, 0, True)
                step(i, 1, True)
            step(NG // 2 - 1, 0, True)
            step(NG // 2 - 1, 1, False)

            for c in range(DC):
                act.wait_ge(acc_added, 4 + 8 * NG)
                if c >= 2:
                    act.wait_ge(sq_used, 2 * DC + c - 1)
                fn(sq3[:, c % 2, :], x1[:, c, :], ACT.Square).then_inc(sq_ready, 1)
            act.wait_ge(sq_used, 3 * DC)
            root(rs3[:, :], "ms3", 0).then_inc(take_sem("ms3"), 1)

        @block.vector
        def _(dve):
            count = [0]

            def tick(ins):
                count[0] += 1
                ins.then_inc(dve_order, 1)

            def after():
                dve.wait_ge(dve_order, count[0])

            tt, tsc, stt = dve.tensor_tensor, dve.tensor_scalar, dve.scalar_tensor_tensor

            def split_l(n):
                if n >= NW:
                    return
                dve.wait_ge(wh_ready, n + 1)
                tt(wL[:, n % WSPL, :, :], wraw[:, n % WRAW, :, :], wH[:, n % WSPL, :, :], ALU.subtract).then_inc(
                    wl_ready, 1)

            tick(dve.memset(shift[:, :, 0:1], 0.0))
            dve.memset(glu[:, :, 0:TAPS - 1], 0.0).then_inc(zero_ready, 1)
            dve.wait_ge(s_cst, 48)
            tick(tsc(omka[:, :], vc("ka", 0, CB), -1.0, 1.0, ALU.mult, ALU.add))
            dve.wait_ge(s_x, 16)
            wait_taken(dve, "ms1")
            tick(dve.reciprocal(rs[:, :], rs[:, :]))
            after()
            for c in range(DC):
                tick(stt(h[:, c, :], xin[:, c, :], vc("gmix", c), rs[:, :], ALU.mult, ALU.mult))
                after()
                tick(dve.tensor_copy(hH[:, c, :], h[:, c, :]))
                after()
                tt(hL[:, c, :], h[:, c, :], hH[:, c, :], ALU.subtract).then_inc(h_split, 1)
            dve.wait_ge(wloh_ready, 1)
            tt(wloL[:, :, :], wlo[:, :, :], wloH[:, :, :], ALU.subtract).then_inc(wlol_ready, 1)
            split_l(0)
            split_l(1)

            wait_taken(dve, "lora_a")
            tick(tt(sdiff[0:64, :], shift[0:64, 0, 0:T], shift[0:64, 0, 1:], ALU.subtract))
            after()
            stt(sgb[0:64, :], sdiff[0:64, :], vc("mua", 0, 1, 64), shift[0:64, 0, 1:], ALU.mult, ALU.add).then_inc(
                lora_shifted, 1)
            dve.wait_ge(lora_shifted, 1)
            tick(dve.tensor_copy(lwa[32:64, :], sgb[32:64, :]))
            dve.wait_ge(lora_ready, 1)
            wait_taken(dve, "lora_b")
            tick(tt(sdiff[0:LG, :], shift[0:LG, 1, 0:T], shift[0:LG, 1, 1:], ALU.subtract))
            after()
            stt(sgb[0:LG, :], sdiff[0:LG, :], vc("mub", 0, 1, LG), shift[0:LG, 1, 1:], ALU.mult, ALU.add).then_inc(
                lora_shifted, 1)
            for n in range(12):
                dst = (r_in, k_in, v_in)[n // 4]
                wait_taken(dve, f"w{n}")
                tick(tt(sdiff[:, :], shift[:, n % 2, 0:T], shift[:, n % 2, 1:], ALU.subtract))
                after()
                stt(dst[:, n % 4, :], sdiff[:, :], vc("mu", n), shift[:, n % 2, 1:], ALU.mult, ALU.add).then_inc(
                    rkv_ready, 1)
                dve.wait_ge(rkv_ready, n + 1)
                split_l(n + 2)
            dve.wait_ge(zero_ready, 1)
            for i in range(CB):
                n = W_CONV + 2 * i
                wait_taken(dve, f"w{n}")
                wait_filled(dve, f"w{n + 1}")
                tt(glu[:, i, TAPS - 1:], ps(f"w{n + 1}")[:, :], sgb[:, :], ALU.mult).then_inc(take_sem(f"w{n + 1}"), 1)
                if n + 3 < W_MIX:
                    split_l(n + 2)
                    split_l(n + 3)
            wait_taken(dve, f"w{W_MIX - 1}")
            done_taps, last_tap = [0], [0]

            def taps(k):
                for _ in range(k):
                    if done_taps[0] == CB * TAPS:
                        return
                    i, j = divmod(done_taps[0], TAPS)
                    done_taps[0] += 1
                    if j == 0:
                        ins = tsc(cy[:, i, :], glu[:, i, 0:T], vc("dw", i * TAPS), vc("dwb", i), ALU.mult, ALU.add)
                    else:
                        dve.wait_ge(dve_order, last_tap[0])
                        ins = stt(cy[:, i, :], glu[:, i, j:j + T], vc("dw", i * TAPS + j), cy[:, i, :],
                                  ALU.mult, ALU.add)
                    if j < TAPS - 1:
                        tick(ins)
                        last_tap[0] = count[0]
                    else:
                        ins.then_inc(conv_out, 1)

            dve.memset(state[:, :, :], 0.0).then_inc(state_ready, 1)

            def flat(a):
                return a.rearrange("p a b -> p (a b)")

            def masked(name, dst, mask, par):
                wait_filled(dve, name)
                m = C(mask).unsqueeze(1).broadcast_to([P, 4, P])
                tt(dst, ps(name)[:, :].rearrange("p (a b) -> p a b", b=P), m, ALU.mult).then_inc(take_sem(name), 1)

            def decays(t):
                tsl, s = slice(t * P, (t + 1) * P), t % 2
                wait_taken(dve, f"zw{t}")
                tick(tsc(flat(ld[:, :, :]), flat(ld[:, :, :]), -float(np.exp(-0.5)), None, ALU.mult))
                after()
                if t >= 2:
                    wait_filled(dve, f"Y{2 * t - 3}")
                tick(dve.tensor_tensor_scan(flat(bb[:, :, :]), rst[:, :], flat(ld[:, :, :]), 0.0, ALU.mult, ALU.add))
                after()
                tt(flat(ex[:, :, :]), flat(bb[:, :, :]), flat(ld[:, :, :]), ALU.subtract).then_inc(cum_ready, 1)
                tt(kn[:, :, :], k_in[:, :, tsl], bc(vc("kk", 0, CB), P), ALU.mult).then_inc(kn_ready, 1)
                wait_taken(dve, f"za{t}")
                for i in range(CB):
                    ins = tsc(k2[:, i, :], aa[:, i, :], vc("ka", i), omka[:, i:i + 1], ALU.mult, ALU.add)
                tick(ins)
                after()
                tick(tt(k2[:, :, :], k_in[:, :, tsl], k2[:, :, :], ALU.mult))
                wait_filled(dve, f"kn{t}")
                tsc(flat(be[:, s]), ps(f"kn{t}")[:, :], 1e-24, None, ALU.max).then_inc(take_sem(f"kn{t}"), 1)
                after()

            def keys_and_rates(t):
                tsl, s = slice(t * P, (t + 1) * P), t % 2
                for i in range(CB):
                    ins = stt(sqh[:, i, :], r_in[:, i, tsl], vc("rk", i), k2[:, i, :], ALU.mult, ALU.mult)
                ins.then_inc(rk_ready, 1)
                dve.wait_ge(kn_root, t + 1)
                tick(dve.reciprocal(flat(be[:, s]), flat(be[:, s])))
                after()
                dve.wait_ge(kn_ready, t + 1)
                tick(stt(flat(kn[:, :, :]), flat(kn[:, :, :]), -1.0, flat(be[:, s]), ALU.mult, ALU.mult))
                after()
                dve.wait_ge(exps_ready, t + 1)
                tick(stt(flat(bb[:, :, :]), flat(kn[:, :, :]), -1.0, flat(aa[:, :, :]), ALU.mult, ALU.mult))
                tt(nkt[:, s], kn[:, :, :], ex[:, :, :], ALU.mult)
                tt(rt[:, s], r_in[:, :, tsl], ep[:, :, :], ALU.mult)

            def scaled(t):
                tsl, s = slice(t * P, (t + 1) * P), t % 2
                tick(tt(kh[:, s], k2[:, :, :], em[:, :, :], ALU.mult))
                tick(dve.tensor_copy(pend[:, s], ep[:, :, CHUNK - 1::CHUNK]))
                after()
                tick(tt(bh[:, s], bb[:, :, :], em[:, :, :], ALU.mult))
                wait_filled(dve, f"rk{t}")
                tt(bonus[:, :, tsl], ps(f"rk{t}")[:, :].rearrange("p (a b) -> p a b", b=P), v_in[:, :, tsl],
                   ALU.mult).then_inc(take_sem(f"rk{t}"), 1)
                after()
                for src, dst in ((bh, be), (kh, ke)):
                    for i in range(CB):
                        pe_ = pend[:, s, i, :].unsqueeze(2).broadcast_to([P, 2, CHUNK])
                        ins = tt(dst[:, s, i, :].rearrange("p (c n) -> p c n", n=CHUNK),
                                 src[:, s, i, :].rearrange("p (c n) -> p c n", n=CHUNK), pe_, ALU.mult)
                ins.then_inc(feats_ready, 1)

            def masks_and_inverse(t):
                s = t % 2
                ident4 = C(C_ID).unsqueeze(1).broadcast_to([P, 4, P])
                for par in range(2):
                    name = f"M{par}_{t}"
                    wait_filled(dve, name)
                    tick(tt(xx[:, par], ps(name)[:, :].rearrange("p (a b) -> p a b", b=P),
                            C(C_E1).unsqueeze(1).broadcast_to([P, 4, P]), ALU.mult))
                    after()
                    tt(nn[:, par], xx[:, par], ident4, ALU.add).then_inc(take_sem(name), 1)
                    taps(1)
                for par in range(2):
                    name = f"MT{par}_{t}"
                    wait_filled(dve, name)
                    tick(tt(lt[:, par], ps(name)[:, :].rearrange("p (a b) -> p a b", b=P),
                            C(C_STRICT).unsqueeze(1).broadcast_to([P, 4, P]), ALU.mult))
                    after()
                    tick(tt(nt[:, s, par], lt[:, par], C(C_E1T).unsqueeze(1).broadcast_to([P, 4, P]), ALU.mult))
                    after()
                    tt(nt[:, s, par], nt[:, s, par], ident4, ALU.add).then_inc(take_sem(name), 1)
                    taps(1)
                for name, dst, mask in (("ak", mak, C_STRICT), ("rb", mrb, C_INCL), ("rq", mrk, C_INCL)):
                    for par in range(2):
                        masked(f"{name}{par}_{t}", dst[:, par] if dst is mak else dst[:, s, par], mask, par)
                        taps(1)
                for lv in range(5):
                    for par in range(2):
                        masked(f"X{lv}{par}_{t}", xx[:, par], (C_E2, C_E4, C_E8, C_E16, C_E32)[lv], par)
                        taps(1)
                    for par in range(2):
                        for name, dst in ((f"N{lv}{par}_{t}", nn[:, par]), (f"NT{lv}{par}_{t}", nt[:, s, par])):
                            if name not in turn:
                                continue
                            wait_filled(dve, name)
                            wait_filled(dve, f"NT{lv}{par}_{t}")
                            tt(dst, ps(name)[:, :].rearrange("p (a b) -> p a b", b=P), dst, ALU.add).then_inc(
                                take_sem(name), 1)
                        taps(1)

            def new_state(c):
                s = (c // 2) % 2
                if c:
                    wait_taken(dve, f"ST{c - 1}")
                else:
                    dve.wait_ge(state_ready, 1)
                tick(tt(sdec[:, :, :], state[:, :, :], bc(pend[:, s, :, c % 2], P), ALU.mult))
                after()
                wait_filled(dve, f"ST{c}")
                wait_filled(dve, f"SA{c}")
                wait_filled(dve, f"Y{c}")
                for par in range(2):
                    rows = slice(HD * par, HD * par + HD)
                    ins = tt(state[rows, :, rows],
                             ps(f"ST{c}")[rows, :].rearrange("p (a b) -> p a b", b=P)[:, :, rows],
                             sdec[rows, :, rows], ALU.add)
                ins.then_inc(take_sem(f"ST{c}"), 1)

            decays(0)
            keys_and_rates(0)
            scaled(0)
            for t in range(TT):
                masks_and_inverse(t)
                if t + 1 < TT:
                    decays(t + 1)
                new_state(2 * t)
                if t + 1 < TT:
                    keys_and_rates(t + 1)
                new_state(2 * t + 1)
                if t + 1 < TT:
                    scaled(t + 1)
            taps(CB * TAPS)

            for c in range(DC):
                dve.wait_ge(h_again, c + 1)
                tt(hL[:, c, :], h[:, c, :], hH[:, c, :], ALU.subtract).then_inc(hl_again, 1)
            split_l(W_MIX)
            split_l(W_MIX + 1)
            dve.wait_ge(conv_out, CB)
            wait_filled(dve, "cmean")
            for i in range(CB):
                tt(cy[:, i, :], cy[:, i, :], ps("cmean")[:, :], ALU.subtract).then_inc(
                    cy_norm if i < CB - 1 else take_sem("cmean"), 1)
            wait_taken(dve, "cmean")
            split_l(W_MIX + 2)
            split_l(W_MIX + 3)
            wait_taken(dve, "cvar")
            tick(dve.reciprocal(rs[:, :], rs[:, :]))
            after()
            for i in range(CB):
                tick(tt(cy[:, i, :], cy[:, i, :], rs[:, :], ALU.mult))
                after()
                tsc(cy[:, i, :], cy[:, i, :], vc("lng", i), vc("lnb", i), ALU.mult, ALU.add).then_inc(cy_norm, 1)
            for i in range(CB):
                wait_filled(dve, f"gmean{i}")
                tt(yt[:, i, :], yt[:, i, :], ps(f"gmean{i}")[:, :], ALU.subtract).then_inc(take_sem(f"gmean{i}"), 1)
                if i in (1, 3):
                    split_l(W_MIX + 4 + i // 2)
                wait_taken(dve, f"gvar{i}")
                tick(dve.reciprocal(ma[:, :], ma[:, :]))
                after()
                tick(tt(yt[:, i, :], yt[:, i, :], ma[:, :], ALU.mult))
                after()
                tick(tsc(yt[:, i, :], yt[:, i, :], vc("gng", i), vc("gnb", i), ALU.mult, ALU.add))
                after()
                tick(tt(yt[:, i, :], yt[:, i, :], bonus[:, i, :], ALU.add))
                after()
                wait_filled(dve, f"gate{i}")
                tt(yt[:, i, :], yt[:, i, :], ps(f"gate{i}")[:, :], ALU.mult).then_inc(take_sem(f"gate{i}"), 1)
                wait_taken(dve, f"gate{i}")
                tick(dve.tensor_copy(oH[:, i, :], yt[:, i, :]))
                after()
                tt(oL[:, i, :], yt[:, i, :], oH[:, i, :], ALU.subtract).then_inc(o_ready, 1)
            for i in range(CB):
                dve.wait_ge(cy_sig, i + 1)
                tick(tt(cy[:, i, :], cy[:, i, :], glu[:, i, 0:T], ALU.mult))
                after()
                tick(dve.tensor_copy(cyH[:, i, :], cy[:, i, :]))
                after()
                tt(cyL[:, i, :], cy[:, i, :], cyH[:, i, :], ALU.subtract).then_inc(cy_ready, 1)
            dve.wait_ge(o_ready, CB)
            for k in range(4, len(MIX_ORDER)):
                kind, d = MIX_ORDER[k]
                if kind != "p":
                    split_l(W_MIX + k + 2)
                    continue
                wait_taken(dve, f"ga{d}")
                wait_filled(dve, f"pw{d}")
                stt(ma[:, :], ps(f"pw{d}")[:, :], vc("pwb", d), sga[:, d % 2, :], ALU.add, ALU.mult).then_inc(
                    take_sem(f"pw{d}"), 1)
                wait_taken(dve, f"gb{d}")
                wait_filled(dve, f"wo{d}")
                tt(mb[:, :], ps(f"wo{d}")[:, :], sgw[:, d % 2, :], ALU.mult).then_inc(take_sem(f"wo{d}"), 1)
                wait_taken(dve, f"pw{d}")
                wait_taken(dve, f"wo{d}")
                tick(tt(mm_[:, :], ma[:, :], mb[:, :], ALU.add))
                after()
                dve.tensor_copy(mixH[:, d, :], mm_[:, :]).then_inc(mix_ready, 1)
                dve.wait_ge(mix_ready, 2 * d + 1)
                tt(mixL[:, d, :], mm_[:, :], mixH[:, d, :], ALU.subtract).then_inc(mix_ready, 1)
                dve.wait_ge(mix_ready, 2 * d + 2)
                split_l(W_MIX + k + 2)
            for d in range(DC):
                dve.wait_ge(xr_loaded, 16)
                wait_filled(dve, f"wout{d}")
                tt(x1[:, d, :], ps(f"wout{d}")[:, :], x1[:, d, :], ALU.add).then_inc(take_sem(f"wout{d}"), 1)
                split_l(W_OUT + d + 2)
            wait_taken(dve, "ms2")
            tick(dve.reciprocal(rs2[:, :], rs2[:, :]))
            after()
            for c in range(DC):
                tick(stt(h2f[:, c % 2, :], x1[:, c, :], vc("gffn", c), rs2[:, :], ALU.mult, ALU.mult))
                after()
                dve.tensor_copy(h2H[:, c, :], h2f[:, c % 2, :]).then_inc(h_split, 1)
                dve.wait_ge(h_split, DC + 2 * c + 1)
                tt(h2L[:, c, :], h2f[:, c % 2, :], h2H[:, c, :], ALU.subtract).then_inc(h_split, 1)
            for m in range(2 * PKH):
                split_l(W_Q + m + 2)
                hd, half = m // 2, m % 2
                wait_filled(dve, f"sc{m}")
                S = [ps(f"sc{m}")[:, t * P:(t + 1) * P] for t in range(TT)]
                v8 = [tv[:, t, half, hd, 0:8] for t in range(TT)]
                w8 = [tv[:, t, half, hd, 8:16] for t in range(TT)]
                for t in range(TT):
                    tick(dve.max(v8[t], S[t]))
                after()
                for t in range(TT):
                    tick(dve.max_index(ti[:, t, half, hd, 0:8], v8[t], S[t]))
                    ins = dve.match_replace(scr[:, t, :], v8[t], S[t], -3.0e38)
                    if t < TT - 1:
                        tick(ins)
                ins.then_inc(take_sem(f"sc{m}"), 1)
                wait_taken(dve, f"sc{m}")
                for t in range(TT):
                    tick(dve.max(w8[t], scr[:, t, :]))
                after()
                for t in range(TT):
                    tick(dve.max_index(ti[:, t, half, hd, 8:16], w8[t], scr[:, t, :]))
            after()
            iota16 = C(C_IOTA)[:, 0:TOPK]
            for t in range(TT):
                tick(tt(cand[:, :, :, :], bc2(tv[:, t, 0], TOPK), bc1(tv[:, t, 1], TOPK), ALU.add))
                after()
                for hd in range(PKH):
                    cd = cand[:, hd].rearrange("p a b -> p (a b)")
                    tick(dve.max(best[:, t, hd, 0:8], cd))
                    after()
                    tick(dve.max_index(ci[:, t, hd, 0:8], best[:, t, hd, 0:8], cd))
                    tick(dve.match_replace(cscr[:, hd % 2, :], best[:, t, hd, 0:8], cd, -3.0e38))
                    after()
                    tick(dve.max(best[:, t, hd, 8:16], cscr[:, hd % 2, :]))
                    after()
                    tick(dve.max_index(ci[:, t, hd, 8:16], best[:, t, hd, 8:16], cscr[:, hd % 2, :]))
                after()
                cflat = ci[:, t].rearrange("p a b -> p (a b)")
                tick(tsc(c1[:, 0, :], cflat, 4, None, ALU.logical_shift_right))
                tick(tsc(c1[:, 1, :], cflat, TOPK - 1, None, ALU.bitwise_and))
                after()
                tick(dve.tensor_copy(cf[:, :, :], c1[:, :, :]))
                tick(dve.tensor_copy(tif[:, :, :, :], ti[:, t]))
                after()
                for j in range(2):
                    tick(tt(oneh[:, :, :], bc(cf[:, j, :], TOPK),
                            iota16.unsqueeze(1).broadcast_to([P, PKH * TOPK, TOPK]), ALU.is_equal))
                    after()
                    tick(tt(oneh[:, :, :].rearrange("p (h k) n -> p h k n", h=PKH),
                            oneh[:, :, :].rearrange("p (h k) n -> p h k n", h=PKH), bc1(tif[:, j], TOPK), ALU.mult))
                    after()
                    tick(dve.tensor_reduce(ee[:, t, j, :], oneh[:, :, :], AX.X, ALU.add))
                    after()
            hk = "p a b c -> p (a b) c"
            rows = best[:, :, :, :].rearrange(hk)
            tick(dve.tensor_copy(gsum[:, :, :], best[:, :, :, 0]))
            after()
            flat_sum = gsum[:, :, :].rearrange("p a b -> p (a b)")
            tt(rows, rows, bc(flat_sum, TOPK), ALU.subtract).then_inc(best_sub, 1)
            dve.wait_ge(best_exp, 1)
            tick(dve.tensor_reduce(flat_sum, rows, AX.X, ALU.add))
            after()
            tick(dve.reciprocal(flat_sum, flat_sum))
            after()
            tt(rows, rows, bc(flat_sum, TOPK), ALU.mult).then_inc(ee_ready, 1)

            for t in range(TT):
                for n in ("e1", "e2", "gt"):
                    wait_taken(dve, f"{n}T{t}")
            def u_low(n, slot):
                dve.wait_ge(uh_ready, n + 1)
                tt(uL[:, slot % 2, :, :], uraw[:, slot, :, :], uH[:, slot % 2, :, :], ALU.subtract).then_inc(
                    ul_ready, 1)

            dve.wait_ge(ul_ready, NPRE // 2 + 1)
            with dve.Fori(0, NPRE // 8) as i:
                for j in range(4):
                    for b in range(4):
                        dve.wait_ge(wmm_done, 16 * i + 4 * j + b + 1)
                        for k in range(4):
                            tok = bass.ds(2 * T_W * i + 16 * j + 4 * b + k, 1)
                            ins = tsc(rh[:, b, k, :], C(C_IOTA), et[:, 0, tok], et[:, 2, tok],
                                      ALU.is_equal, ALU.mult)
                        tsc(oh2[:, b, 3, :], C(C_IOTA), et[:, 1, tok], None, ALU.is_equal).then_inc(rh_ready, 1)
                        if b == 2:
                            u_low(NPRE // 2 + 4 * i + j + 1, (j + 1) % 4)

            def weigh(q, lap, par, g):
                if g == 0:
                    dve.wait_ge(wg_loaded[par], 32 * lap + 32)
                if g >= PRE:
                    dve.wait_ge(gelu_ready, NPRE + 2 * q + g - PRE + 3)
                if not (isinstance(q, int) and q == 0 and g < 2):
                    dve.wait_ge(al_ready, G * q + g - 1)
                src = gl[:, par, g, :] if g < PRE else ge[:, g - PRE, :]
                tt(af[:, g % 2, :].rearrange("p (b t) -> p b t", t=T_W), src.rearrange("p (b t) -> p b t", t=T_W),
                   wg[:, par, :, g, :], ALU.mult).then_inc(act_ready, 1)

            def a_low(q, par, g):
                dve.wait_ge(ah_ready, G * q + g + 1)
                tt(aL[:, par * G + g, :], af[:, g % 2, :], aH[:, par * G + g, :], ALU.subtract).then_inc(al_ready, 1)

            def v_low(q, u):
                dve.wait_ge(vh_ready, 2 * G * q + u + 1)
                tt(vL[:, u % 4, :], vraw[:, u // G, u % G, :], vH[:, u % 4, :], ALU.subtract).then_inc(vl_ready, 1)

            def add_up(q, sweep):
                for j in range(4):
                    dve.wait_ge(sweep_done, 8 * q + 4 * sweep + j + 1)
                    dst = x1[:, 4 * sweep + j, :]
                    tt(dst, bank[j][:, :], dst, ALU.add).then_inc(acc_added, 1)

            dve.sem_inc(acc_added, 4)
            u_low(NPRE + 1, 1)
            weigh(0, 0, 0, 0)
            weigh(0, 0, 0, 1)
            a_low(0, 0, 0)
            a_low(0, 0, 1)
            weigh(0, 0, 0, 2)
            a_low(0, 0, 2)
            for u in range(4):
                v_low(0, u)

            def step(i, par, more):
                q = 2 * i + par
                base = 2 * (1 - par)
                weigh(q, i, par, G - 1)
                if more:
                    u_low(NPRE + 2 * (q + 1), base)
                a_low(q, par, G - 1)
                for u in (4, 5, 6):
                    v_low(q, u)
                add_up(q, 0)
                v_low(q, 7)
                if more:
                    nq, nlap, npar = q + 1, i + par, 1 - par
                    weigh(nq, nlap, npar, 0)
                    weigh(nq, nlap, npar, 1)
                    a_low(nq, npar, 0)
                    a_low(nq, npar, 1)
                    u_low(NPRE + 2 * nq + 1, base + 1)
                    weigh(nq, nlap, npar, 2)
                    a_low(nq, npar, 2)
                    for u in (0, 1, 2):
                        v_low(nq, u)
                add_up(q, 1)
                if more:
                    v_low(nq, 3)

            with dve.Fori(0, NG // 2 - 1) as i:
                step(i, 0, True)
                step(i, 1, True)
            step(NG // 2 - 1, 0, True)
            step(NG // 2 - 1, 1, False)

            dve.wait_ge(acc_added, 4 + 8 * NG)
            wait_taken(dve, "ms3")
            tick(dve.reciprocal(rs3[:, :], rs3[:, :]))
            after()
            for c in range(DC):
                if c >= 2:
                    dve.wait_ge(y_stored[c % 2], 16 * (c // 2))
                stt(yo[:, c % 2, :], x1[:, c, :], vc("gf", c), rs3[:, :], ALU.mult, ALU.mult).then_inc(y_ready, 1)

        @block.gpsimd
        def _(pool):
            pool.wait_ge(hl_again, DC)
            pool.dma_start(x1[:, :, :], xT).then_inc(xr_loaded, 16)
            wait_taken(pool, f"wout{DC - 1}")
            pool.dma_start(keys[:, :, :], keysT).then_inc(s_keys, 16)

            def u_low(n, slot):
                pool.wait_ge(uh_ready, n + 1)
                pool.tensor_tensor(uL[:, slot % 2, :, :], uraw[:, slot, :, :], uH[:, slot % 2, :, :],
                                   ALU.subtract).then_inc(ul_ready, 1)

            u_low(0, 0)
            with pool.Fori(0, NPRE // 8) as i:
                for j in range(4):
                    u_low(4 * i + j + 1, (j + 1) % 4)
            for t in range(TT):
                wait_taken(pool, f"e2T{t}")
            with pool.Fori(0, NPRE // 8) as i:
                pool.tensor_copy(e2s[:, :], et[:, 1, bass.ds(2 * T_W * i, 2 * T_W)]).then_inc(pool_order, 1)
                pool.wait_ge(pool_order, i + 1)
                for j in range(4):
                    for b in range(4):
                        pool.wait_ge(wmm_done, 16 * i + 4 * j + b + 1)
                        pool.sem_inc(batch_begun, 1)
                        for k in range(3):
                            tok = 16 * j + 4 * b + k
                            ins = pool.tensor_scalar(oh2[:, b, k, :], C(C_IOTA), e2s[:, tok:tok + 1], None,
                                                     ALU.is_equal)
                        ins.then_inc(oh2_ready, 1)
                pool.wait_ge(oh2_ready, 16 * i + 16)


def constants():
    i, j = np.arange(P)[:, None], np.arange(P)[None, :]
    c = np.zeros((NCONST, P, P), np.float32)
    c[C_ID] = i == j
    c[C_M1024], c[C_M512] = 1.0 / D, 1.0 / 512
    c[C_HEAD1] = i // HD == j // HD
    c[C_HEADM] = c[C_HEAD1] / HD
    same = i // CHUNK == j // CHUNK
    c[C_STRICT], c[C_INCL] = same & (i < j), same & (i <= j)
    for k, b in ((C_E1, 1), (C_E2, 2), (C_E4, 4), (C_E8, 8), (C_E16, 16), (C_E32, 32)):
        c[k] = (i // (2 * b) == j // (2 * b)) & (i % (2 * b) >= b) & (j % (2 * b) < b)
    c[C_E1T] = c[C_E1].T
    c[C_IOTA] = j + 0 * i
    reset = np.broadcast_to((np.arange(T) % CHUNK != 0).astype(np.float32), (P, T))
    return np.ascontiguousarray(c.transpose(1, 0, 2)), np.ascontiguousarray(reset)


def columns(v):
    return np.asarray(v).reshape(-1, P).T


def kernel(x, norm_mix_g, w_in, conv_dw, conv_dw_b, conv_ln_g, conv_ln_b, conv_pw, conv_pw_b,
           rw_mu, rw_w0, rw_w2, rw_a0, rw_a2, rw_g2, rw_k_k, rw_k_a, rw_r_k, rw_gn_g, rw_gn_b,
           rw_w_o, w_out, norm_ffn_g, peer_wq, peer_keys, peer_u, peer_v, norm_f_g):
    import concourse.bacc as bacc
    from concourse.bass_utils import run_bass_kernel_spmd

    def pad(v):
        return np.pad(np.asarray(v), (0, P - len(v)))[:, None]

    def blocks(w):
        w = np.asarray(w)
        return w.reshape(w.shape[0] // P, P, w.shape[1] // P, P).transpose(2, 1, 0, 3)

    w = np.asarray(w_in)[0]
    r0 = 2 * 512
    lo0, ga0 = r0 + 3 * 512, r0 + 3 * 512 + LW + LA + LG
    conv = blocks(w[:, :r0])
    order = [blocks(w[:, r0:lo0])]
    for i in range(CB):
        order += [conv[CB + i][None], conv[i][None]]
    ga, gb = blocks(w[:, ga0:ga0 + D]), blocks(w[:, ga0 + D:])
    pw, wo = blocks(conv_pw[0]), blocks(rw_w_o[0])
    for kind, d in MIX_ORDER:
        order += [(ga if kind == "a" else gb)[d][None] if kind != "p" else np.concatenate([pw[d], wo[d]], 1)[None]]
    order += [blocks(w_out[0]), blocks(peer_wq[0])]
    mu = np.asarray(rw_mu)[0]
    dw = np.asarray(conv_dw)[0].reshape(TAPS, CB, P).transpose(2, 1, 0).reshape(P, CB * TAPS)
    cols = {"gmix": columns(norm_mix_g[0]), "dw": dw, "dwb": columns(conv_dw_b[0]), "lng": columns(conv_ln_g[0]),
            "lnb": columns(conv_ln_b[0]), "pwb": columns(conv_pw_b[0]), "mu": columns(mu[:1536]),
            "mua": pad(mu[1536:1600]), "mub": pad(mu[1600:1696]), "w0": columns(rw_w0[0]), "a0": columns(rw_a0[0]),
            "kk": columns(rw_k_k[0]), "ka": columns(rw_k_a[0]), "rk": columns(np.asarray(rw_r_k)[0].reshape(-1)),
            "gng": columns(rw_gn_g[0]), "gnb": columns(rw_gn_b[0]), "gffn": columns(norm_ffn_g[0]),
            "gf": columns(norm_f_g), "eps": np.full((P, 3), (NORM_EPS, LN_EPS, GN_EPS), np.float32)}
    consts, reset = constants()
    arrays = {
        "xT": np.asarray(x)[0].T.reshape(DC, P, T).transpose(1, 0, 2),
        "consts": consts,
        "reset": reset,
        "vecs": np.concatenate([cols[n] for n, _ in VEC], 1),
        "wlora": w[:, lo0:ga0].reshape(DC, P, LW + LA + LG).transpose(1, 0, 2),
        "wall": np.concatenate(order, 0),
        "w2a2": np.concatenate([np.asarray(rw_w2)[0], np.asarray(rw_a2)[0]], 0),
        "g2": np.asarray(rw_g2)[0],
        "keysT": np.asarray(peer_keys)[0].reshape(2 * PKH, NK, P).transpose(2, 0, 1),
        "uT": np.asarray(peer_u)[0].reshape(NK, NK, DC, P).transpose(0, 3, 2, 1),
        "v_tab": np.asarray(peer_v)[0],
    }
    nc = bacc.Bacc("TRN2", target_bir_lowering=False, num_devices=1)
    args = {}
    for name, a in arrays.items():
        arrays[name] = a = np.ascontiguousarray(a)
        args[name] = nc.dram_tensor(name, a.shape, mybir.dt.from_np(a.dtype), kind="ExternalInput").ap()
    args["w_dram"] = nc.dram_tensor("w_dram", (NTB, P, NK, T_W), F32, kind="Internal").ap()
    args["g_dram"] = nc.dram_tensor("g_dram", (NPRE, P, T), F32, kind="Internal").ap()
    args["yT"] = nc.dram_tensor("yT", (DC, P, T), F32, kind="ExternalOutput").ap()
    build(nc, **args)
    r = run_bass_kernel_spmd(nc, [arrays], core_ids=[0])
    return r.results[0]["yT"].reshape(D, T).T.reshape(1, T, D)
```

```python
from contextlib import ExitStack

import numpy as np

import concourse.bass as bass
from concourse import mybir

F32 = mybir.dt.float32
F32R = mybir.dt.float32r
U32 = mybir.dt.uint32
ALU = mybir.AluOpType
ACT = mybir.ActivationFunctionType
AX = mybir.AxisListType

P = 128
D, T = 1024, 512
DC = D // P
CB = 512 // P
TAPS = 31
HEADS, HD = 8, 64
CHUNK = 64
TT = T // P
LW, LA, LG = 32, 32, 96
PKH, TOPK, NK = 8, 16, 128
NORM_EPS, LN_EPS, GN_EPS = 1e-6, 1e-5, 64e-5

C_ID, C_M1024, C_M512, C_HEAD1, C_HEADM, C_STRICT, C_INCL, C_E1, C_E1T, C_E2, C_E4, C_E8, C_E16, C_E32, \
    C_IOTA = range(15)
NCONST = 15
VEC = [("gmix", DC), ("dw", CB * TAPS), ("dwb", CB), ("lng", CB), ("lnb", CB), ("pwb", DC), ("mu", 12),
       ("mua", 1), ("mub", 1), ("w0", CB), ("a0", CB), ("kk", CB), ("ka", CB), ("rk", CB), ("gng", CB),
       ("gnb", CB), ("gffn", DC), ("gf", DC), ("eps", 3)]
VOFF = {}
_o = 0
for _n, _c in VEC:
    VOFF[_n] = _o
    _o += _c
NVEC = _o

W_RKV, W_CONV, W_MIX, W_OUT, W_Q = 0, 12, 20, 44, 52
NW = 68
WRAW, WSPL = 4, 2

MIX_ORDER = [("a", 0), ("b", 0), ("a", 1), ("b", 1)]
for _d in range(DC):
    MIX_ORDER += [("p", _d)] + ([("a", _d + 2), ("b", _d + 2)] if _d + 2 < DC else [])

G = 4
PRE = 2
NG = NK // G
T_W = 32
NTB = T // T_W
NPRE = PRE * NG
KB = 1024


def build(nc, xT, consts, reset, vecs, wlora, wall, w2a2, g2, keysT, uT, v_tab, w_dram, g_dram, yT):
    def at(name, kb, shape, dt=F32):
        return nc.alloc_sbuf_tensor_at(name, shape, dt, offset=16512 + int(kb * KB))

    cst = at("cst", 0, [P, NCONST, P])
    rst = at("rst", 7.5, [P, T])
    vec = at("vec", 9.5, [P, NVEC])
    omka = at("omka", 10.5, [P, CB])
    h = at("h", 12, [P, DC, T])
    wraw = at("wraw", 28, [P, WRAW, DC, P])
    r_in = at("r_in", 44, [P, CB, T])
    k_in = at("k_in", 52, [P, CB, T])
    v_in = at("v_in", 60, [P, CB, T])
    lwa = at("lwa", 68, [LW + LA, T])
    lgs = at("lgs", 70, [LG, T])
    glu = at("glu", 72, [P, CB, TAPS - 1 + T])
    cy = at("cy", 81, [P, CB, T])
    w2a2_s = at("w2a2_s", 89, [LW + LA, 512])
    g2_s = at("g2_s", 91, [LG, 512])
    x1 = at("x1", 191, [P, DC, T])
    xin = at("xin", 159, [P, DC, T])
    hH = at("hH", 93, [P, DC, T], F32R)
    hL = at("hL", 109, [P, DC, T], F32R)
    wH = at("wH", 141, [P, WSPL, DC, P], F32R)
    wL = at("wL", 149, [P, WSPL, DC, P], F32R)
    wlo = at("wlo", 125, [P, DC, LW + LA + LG])
    wloH = at("wloH", 130.25, [P, DC, LW + LA + LG], F32R)
    wloL = at("wloL", 135.5, [P, DC, LW + LA + LG], F32R)
    sq = at("sq", 175, [P, 2, T])
    rs = at("rs", 179, [P, T])
    shift = at("shift", 181, [P, 2, T + 1])
    sdiff = at("sdiff", 185.25, [P, T])
    sgb = at("sgb", 187.5, [P, T])
    nkt = at("nkt", 159, [P, 2, CB, P])
    bh = at("bh", 163, [P, 2, CB, P])
    kh = at("kh", 167, [P, 2, CB, P])
    rt = at("rt", 171, [P, 2, CB, P])
    be = at("be", 175, [P, 2, CB, P])
    ke = at("ke", 191, [P, 2, CB, P])
    ld = at("ld", 125, [P, CB, P])
    ep = at("ep", 127, [P, CB, P])
    em = at("em", 129, [P, CB, P])
    ex = at("ex", 131, [P, CB, P])
    aa = at("aa", 133, [P, CB, P])
    kn = at("kn", 135, [P, CB, P])
    k2 = at("k2", 137, [P, CB, P])
    bb = at("bb", 139, [P, CB, P])
    sqh = at("sqh", 179, [P, CB, P])
    pend = at("pend", 202, [P, 2, CB, 2])
    tok = [at(n, 93 + 4 * i, [P, 2, CB * P]) for i, n in enumerate(["v_tok", "be_tok", "ke_tok", "nkt_tok"])]
    v_tok, be_tok, ke_tok, nkt_tok = tok
    lt = at("lt", 109, [P, 2, 4, P])
    nn = at("nn", 113, [P, 2, 4, P])
    xx = at("xx", 117, [P, 2, 4, P])
    mak = at("mak", 121, [P, 2, 4, P])
    nt = at("nt", 141, [P, 2, 2, 4, P])
    mrb = at("mrb", 149, [P, 2, 2, 4, P])
    mrk = at("mrk", 181, [P, 2, 2, 4, P])
    w1t = at("w1t", 157, [P, CB, P])
    mv = at("mv", 189, [P, 512])
    tapped = at("tapped", 195, [P, 2, T])
    sa = at("sa", 199, [P, 512])
    state = at("state", 203, [P, CB, P])
    sdec = at("sdec", 205, [P, CB, P])
    yt = r_in
    bonus = k_in
    cyH = at("cyH", 125, [P, CB, T], F32R)
    cyL = at("cyL", 133, [P, CB, T], F32R)
    oH = at("oH", 157, [P, CB, T], F32R)
    oL = at("oL", 165, [P, CB, T], F32R)
    mixH = at("mixH", 173, [P, DC, T], F32R)
    mixL = at("mixL", 44, [P, DC, T], F32R)
    sga = at("sga", 60, [P, 2, T])
    sgw = at("sgw", 64, [P, 2, T])
    ma = at("ma", 68, [P, T])
    mb = at("mb", 72, [P, T])
    mm_ = at("mm_", 74, [P, T])
    gsq = at("gsq", 173, [P, CB, T])
    gdev = at("gdev", 181, [P, CB, T])
    cdev = at("cdev", 189, [P, T])
    h2H = at("h2H", 93, [P, DC, T], F32R)
    h2L = at("h2L", 109, [P, DC, T], F32R)
    qt = at("qt", 44, [P, 2, T])
    keys = at("keys", 48, [P, 2 * PKH, NK])
    tv = at("tv", 56, [P, TT, 2, PKH, TOPK])
    ti = at("ti", 60, [P, TT, 2, PKH, TOPK], U32)
    scr = at("scr", 64, [P, TT, NK])
    sq2 = at("sq2", 66, [P, 2, T])
    rs2 = at("rs2", 70, [P, T])
    h2f = at("h2f", 72, [P, 2, T])
    cand = at("cand", 125, [P, PKH, TOPK, TOPK])
    cscr = at("cscr", 133, [P, 2, TOPK * TOPK])
    oneh = at("oneh", 157, [P, PKH * TOPK, TOPK])
    best = at("best", 165, [P, TT, PKH, TOPK])
    ci = at("ci", 167, [P, TT, PKH, TOPK], U32)
    c1 = at("c1", 169, [P, 2, P], U32)
    cf = at("cf", 170, [P, 2, P])
    tif = at("tif", 171, [P, 2, PKH, TOPK])
    ee = at("ee", 172, [P, TT, 2, P])
    gsum = at("gsum", 176, [P, TT, PKH])
    et = at("et", 176.25, [P, 3, T])
    e2s = at("e2s", 186.25, [P, 2 * T_W])
    oh2 = at("oh2", 60, [P, 4, 4, P])
    rh = at("rh", 68, [P, 4, 4, P])
    wst = at("wst", 125, [P, 2, NK, T_W])
    uraw = at("uraw", 12, [P, G, DC, P])
    uH = at("uH", 28, [P, 2, DC, P], F32R)
    uL = at("uL", 36, [P, 2, DC, P], F32R)
    vraw = at("vraw", 44, [P, 2, G, 512])
    vH = at("vH", 60, [P, 4, 512], F32R)
    vL = at("vL", 68, [P, 4, 512], F32R)
    ge = at("ge", 84, [P, 2, T])
    af = at("af", 157, [P, 2, T])
    gl = at("gl", 161, [P, 2, PRE, T])
    wg = at("wg", 169, [P, 2, NTB, G, T_W])
    aH = at("aH", 125, [P, 2 * G, T], F32R)
    aL = at("aL", 141, [P, 2 * G, T], F32R)
    sq3 = at("sq3", 16, [P, 2, T])
    rs3 = at("rs3", 20, [P, T])

    def C(i):
        return cst[:, i, :]

    def vc(name, i=0, n=1, rows=P):
        o = VOFF[name] + i
        return vec[0:rows, o:o + n]

    def bc1(a, n):
        return a.unsqueeze(2).broadcast_to([P, a.shape[1], n, a.shape[2]])

    def bc2(a, n):
        return a.unsqueeze(3).broadcast_to([P, a.shape[1], a.shape[2], n])

    def bc(col, n):
        return col.unsqueeze(2).broadcast_to([P, col.shape[1], n])

    with ExitStack() as ctx:
        def sem(name):
            return ctx.enter_context(nc.semaphore(name))

        bank = [ctx.enter_context(nc.psum_tensor(f"bank{i}", [P, 512], F32)) for i in range(8)]
        filled = [sem(f"bank{i}_filled") for i in range(8)]
        taken = [sem(f"bank{i}_taken") for i in range(8)]
        turn = {}
        fills, takes = [0] * 8, [0] * 8

        s_cst, s_lora, s_small, s_keys = (sem(n) for n in
                                          ["cst_loaded", "lora_loaded", "small_loaded", "keys_loaded"])
        s_x = [sem(f"x{i}_loaded") for i in range(2)]
        sum_grown = sem("sum_grown")
        w_loaded = [sem(f"w{i}_loaded") for i in range(WRAW)]
        wh_ready, wl_ready = sem("wh_ready"), sem("wl_ready")
        wloh_ready, wlol_ready = sem("wloh_ready"), sem("wlol_ready")
        dve_order, pool_order = sem("dve_order"), sem("pool_order")
        h_new, h_high, h_split = sem("h_new"), sem("h_high"), sem("h_split")
        sq_ready = sem("sq_ready")
        zero_ready = sem("zero_ready")
        rkv_ready = sem("rkv_ready")
        lora_shifted, lora_ready = sem("lora_shifted"), sem("lora_ready")
        conv_out, conv_last, cy_sq = sem("conv_out"), sem("conv_last"), sem("cy_sq")
        cy_part, o_high = sem("cy_part"), sem("o_high")
        cy_norm, cy_sig, cy_ready = sem("cy_norm"), sem("cy_sig"), sem("cy_ready")
        kn_root = sem("kn_root")
        cum_ready, exps_ready, kn_ready, sqk_ready = (sem(n) for n in [
            "cum_ready", "exps_ready", "kn_ready", "sqk_ready"])
        rk_ready, feats_ready, state_ready = sem("rk_ready"), sem("feats_ready"), sem("state_ready")
        hl_again, ysq_ready, o_ready, h_again = (sem(n) for n in ["hl_again", "ysq_ready", "o_ready", "h_again"])
        mix_ready, xr_loaded = sem("mix_ready"), sem("xr_loaded")
        best_sub, best_exp, oh2_ready, batch_begun = (sem(n) for n in [
            "best_sub", "best_exp", "oh2_ready", "batch_begun"])
        g_stored = [sem(f"g{i}_stored") for i in range(2)]
        ee_ready = sem("ee_ready")
        rh_ready, wmm_done, wst_ready = sem("rh_ready"), sem("wmm_done"), sem("wst_ready")
        wst_stored = [sem(f"wst{i}_stored") for i in range(2)]
        u_loaded = [sem(f"u{i}_loaded") for i in range(G)]
        v_loaded = [sem(f"v{i}_loaded") for i in range(2 * G)]
        wg_loaded = [sem(f"wg{i}_loaded") for i in range(2)]
        uh_ready, ul_ready, scores_done, gelu_ready = (sem(n) for n in [
            "uh_ready", "ul_ready", "scores_done", "gelu_ready"])
        act_ready, ah_ready, al_ready = sem("act_ready"), sem("ah_ready"), sem("al_ready")
        vh_ready, vl_ready, unit_done, sweep_done, acc_added = (sem(n) for n in [
            "vh_ready", "vl_ready", "unit_done", "sweep_done", "acc_added"])
        y_ready, y_stored = sem("y_ready"), [sem(f"y{i}_stored") for i in range(2)]

        GROUP_BANKS = (0, 1, 5, 6)
        block = ctx.enter_context(nc.Block())

        def wait_filled(eng, name):
            eng.wait_ge(filled[turn[name][0]], turn[name][1])

        def wait_taken(eng, name):
            eng.wait_ge(taken[turn[name][0]], turn[name][2])

        def fill_sem(name):
            return filled[turn[name][0]]

        def take_sem(name):
            return taken[turn[name][0]]

        def ps(name):
            return bank[turn[name][0]]

        @block.tensor
        def _(pe):
            def begin(name, b):
                if takes[b]:
                    pe.wait_ge(taken[b], takes[b])
                fills[b] += 1
                takes[b] += 1
                turn[name] = (b, fills[b], takes[b])
                return bank[b]

            def mm(out, lhsT, rhs, start=True, stop=True):
                return pe.matmul(out, lhsT, rhs, start=start, stop=stop, skip_group_check=True)

            def mm3(out, lH, lL, rH, rL, first, last):
                mm(out, lH, rH, first, False)
                mm(out, lH, rL, False, False)
                return mm(out, lL, rH, False, last)

            def project(name, b, n, xH, xL, splits=None):
                o = begin(name, b)
                pe.wait_ge(wl_ready, n + 1)
                for c in range(DC):
                    if splits is not None:
                        pe.wait_ge(h_split, splits + c + 1)
                    last = mm3(o[:, :], wH[:, n % WSPL, c, :], wL[:, n % WSPL, c, :], xH[:, c, :], xL[:, c, :],
                               c == 0, c == DC - 1)
                last.then_inc(fill_sem(name), 1)

            def mean_square(name, b, total, nth):
                o = begin(name, b)
                pe.wait_ge(sum_grown, (nth + 1) * DC)
                mm(o[:, :], C(C_M1024), total[:, :]).then_inc(filled[b], 1)

            pe.wait_ge(s_cst, 48)
            mean_square("ms1", 0, rs, 0)

            pe.wait_ge(wlol_ready, 1)
            for name, b, lo, n in (("lora_a", 1, 0, LW + LA), ("lora_b", 2, LW + LA, LG)):
                o = begin(name, b)
                for c in range(DC):
                    pe.wait_ge(h_split, c + 1)
                    last = mm3(o[0:n, :], wloH[:, c, lo:lo + n], wloL[:, c, lo:lo + n], hH[:, c, :], hL[:, c, :],
                               c == 0, c == DC - 1)
                last.then_inc(fill_sem(name), 1)
            for n in range(W_CONV):
                project(f"w{n}", (3, 1)[n % 2], n, hH, hL)

            ring = [0]

            def tile_bank():
                ring[0] += 1
                return ring[0] % 5

            def low_rank(t, banks=None):
                ts_ = slice(t * P, (t + 1) * P)
                for k, (name, r0, r1) in enumerate((("zw", 0, LW), ("za", LW, LW + LA))):
                    o = begin(f"{name}{t}", banks[k] if banks else tile_bank())
                    for i in range(CB):
                        last = mm(o[:, i * P:(i + 1) * P], w2a2_s[r0:r1, i * P:(i + 1) * P], lwa[r0:r1, ts_])
                    last.then_inc(fill_sem(f"{name}{t}"), 1)

            def head_sum(name, s, t, b=None):
                o = begin(f"{name}{t}", tile_bank() if b is None else b)
                pe.wait_ge(s, t + 1)
                mm(o[:, :], C(C_HEAD1), sqh[:, :, :].rearrange("p a b -> p (a b)")).then_inc(
                    fill_sem(f"{name}{t}"), 1)

            def token_major(t):
                pe.wait_ge(feats_ready, t + 1)
                for name, src in (("nkt", nkt[:, t % 2]), ("v", v_in[:, :, t * P:(t + 1) * P]),
                                  ("be", be[:, t % 2]), ("ke", ke[:, t % 2])):
                    o = begin(f"{name}T{t}", tile_bank())
                    for i in range(CB):
                        last = pe.transpose(o[:, i * P:(i + 1) * P], src[:, i, :], C(C_ID))
                    last.then_inc(fill_sem(f"{name}T{t}"), 1)

            def products(t):
                pe.wait_ge(feats_ready, t + 1)
                f = {"n": nkt, "b": bh, "k": kh, "r": rt}
                for name, l, r in (("M", "n", "b"), ("MT", "b", "n"), ("ak", "k", "n"), ("rb", "b", "r"),
                                   ("rq", "k", "r")):
                    for par in range(2):
                        rows = slice(HD * par, HD * par + HD)
                        o = begin(f"{name}{par}_{t}", tile_bank())
                        for i in range(CB):
                            last = mm(o[:, i * P:(i + 1) * P], f[l][rows, t % 2, i, :], f[r][rows, t % 2, i, :])
                        last.then_inc(fill_sem(f"{name}{par}_{t}"), 1)

            def invert(t):
                for lv in range(5):
                    for par in range(2):
                        o = begin(f"X{lv}{par}_{t}", tile_bank())
                        wait_taken(pe, f"MT{par}_{t}")
                        wait_taken(pe, f"M{par}_{t}" if lv == 0 else f"N{lv - 1}{par}_{t}")
                        for i in range(4):
                            last = mm(o[:, i * P:(i + 1) * P], lt[:, par, i, :], nn[:, par, i, :])
                        last.then_inc(fill_sem(f"X{lv}{par}_{t}"), 1)
                    for par in range(2):
                        wait_taken(pe, f"X{lv}{par}_{t}")
                        if lv:
                            wait_taken(pe, f"NT{lv - 1}{par}_{t}")
                        if lv < 4:
                            o = begin(f"N{lv}{par}_{t}", tile_bank())
                            for i in range(4):
                                last = mm(o[:, i * P:(i + 1) * P], nt[:, t % 2, par, i, :], xx[:, par, i, :])
                            last.then_inc(fill_sem(f"N{lv}{par}_{t}"), 1)
                        o = begin(f"NT{lv}{par}_{t}", tile_bank())
                        for i in range(4):
                            last = mm(o[:, i * P:(i + 1) * P], xx[:, par, i, :], nt[:, t % 2, par, i, :])
                        last.then_inc(fill_sem(f"NT{lv}{par}_{t}"), 1)

            def solved(t):
                o = begin(f"W1{t}", tile_bank())
                wait_taken(pe, f"nktT{t}")
                for par in range(2):
                    wait_taken(pe, f"NT4{par}_{t}")
                    for i in range(CB):
                        c = (2 * i + par) * HD
                        last = mm(o[HD * par:HD * par + HD, i * P:(i + 1) * P], nkt_tok[:, t % 2, c:c + HD],
                                  nt[:, t % 2, par, i, :])
                last.then_inc(fill_sem(f"W1{t}"), 1)
                o = begin(f"MV{t}", tile_bank())
                wait_taken(pe, f"vT{t}")
                for par in range(2):
                    wait_taken(pe, f"ak{par}_{t}")
                    for i in range(CB):
                        c = (2 * i + par) * HD
                        last = mm(o[:, c:c + HD], mak[:, par, i, :], v_tok[:, t % 2, c:c + HD])
                last.then_inc(fill_sem(f"MV{t}"), 1)

            def chunk(c):
                t, rows = c // 2, slice(CHUNK * (c % 2), CHUNK * (c % 2) + CHUNK)
                o = begin(f"SA{c}", 5)
                wait_taken(pe, f"MV{t}")
                wait_taken(pe, f"W1{t}")
                for par in range(2):
                    for i in range(CB):
                        q = (2 * i + par) * HD
                        mm(o[rows, q:q + HD], nt[:, t % 2, par, i, rows], mv[:, q:q + HD],
                           par == 0 and i == 0, False)
                if c:
                    wait_taken(pe, f"ST{c - 1}")
                else:
                    pe.wait_ge(state_ready, 1)
                for i in range(CB):
                    last = mm(o[rows, i * P:(i + 1) * P], w1t[:, i, rows], state[:, i, :], False, i == CB - 1)
                last.then_inc(fill_sem(f"SA{c}"), 1)
                st = begin(f"ST{c}", 6)
                wait_taken(pe, f"keT{t}")
                for i in range(CB):
                    q = slice(i * P, (i + 1) * P)
                    mm(st[:, q], ke_tok[rows, t % 2, q], v_tok[rows, t % 2, q], i == 0, False)
                y = begin(f"Y{c}", 7)
                for i in range(CB):
                    mm(y[:, i * CHUNK:(i + 1) * CHUNK], state[:, i, :], rt[:, t % 2, i, rows], i == 0, False)
                wait_taken(pe, f"beT{t}")
                wait_taken(pe, f"SA{c}")
                for i in range(CB):
                    q = slice(i * P, (i + 1) * P)
                    last = mm(st[:, q], be_tok[rows, t % 2, q], sa[rows, q], False, i == CB - 1)
                last.then_inc(fill_sem(f"ST{c}"), 1)
                for par in range(2):
                    wait_taken(pe, f"rb{par}_{t}")
                    wait_taken(pe, f"rq{par}_{t}")
                    for i in range(CB):
                        q = slice((2 * i + par) * HD, (2 * i + par + 1) * HD)
                        yo_ = y[HD * par:HD * par + HD, i * CHUNK:(i + 1) * CHUNK]
                        mm(yo_, v_tok[rows, t % 2, q], mrk[rows, t % 2, par, i, rows], False, False)
                        last = mm(yo_, sa[rows, q], mrb[rows, t % 2, par, i, rows], False, True)
                last.then_inc(fill_sem(f"Y{c}"), 1)

            for n in range(W_CONV, W_MIX):
                project(f"w{n}", (3, 1)[n % 2], n, hH, hL)
                if n == W_CONV:
                    pe.wait_ge(lora_ready, 2)
                    pe.wait_ge(s_small, 32)
                    low_rank(0, (0, 2))
                elif n == W_CONV + 2:
                    head_sum("kn", sqk_ready, 0, 4)
                elif n == W_CONV + 4:
                    head_sum("rk", rk_ready, 0, 5)
            token_major(0)
            for t in range(TT):
                more = t + 1 < TT
                products(t)
                invert(t)
                if more:
                    low_rank(t + 1)
                solved(t)
                if more:
                    head_sum("kn", sqk_ready, t + 1)
                chunk(2 * t)
                if more:
                    head_sum("rk", rk_ready, t + 1)
                chunk(2 * t + 1)
                if more:
                    token_major(t + 1)

            def mix_block(k):
                kind, d = MIX_ORDER[k]
                n = W_MIX + k
                if kind != "p":
                    project(f"g{kind}{d}", 3 if kind == "a" else 4, n, hH, hL)
                    return
                pe.wait_ge(wl_ready, n + 1)
                for name, b, c0, xH, xL, ready in ((f"pw{d}", 5, 0, cyH, cyL, cy_ready),
                                                   (f"wo{d}", 6, CB, oH, oL, o_ready)):
                    o = begin(name, b)
                    for c in range(CB):
                        if d == 0:
                            pe.wait_ge(ready, c + 1)
                        last = mm3(o[:, :], wH[:, n % WSPL, c0 + c, :], wL[:, n % WSPL, c0 + c, :],
                                   xH[:, c, :], xL[:, c, :], c == 0, c == CB - 1)
                    last.then_inc(fill_sem(name), 1)

            o = begin("cmean", 2)
            for i in range(CB):
                if i < CB - 1:
                    pe.wait_ge(conv_out, i + 1)
                else:
                    pe.wait_ge(conv_last, 1)
                last = mm(o[:, :], C(C_M512), cy[:, i, :], i == 0, i == CB - 1)
            last.then_inc(filled[2], 1)
            wait_taken(pe, f"Y{2 * TT - 1}")
            for i, b in enumerate(GROUP_BANKS):
                o = begin(f"gmean{i}", b)
                mm(o[:, :], C(C_HEADM), yt[:, i, :]).then_inc(filled[b], 1)
            o = begin("cvar", 2)
            for i in range(CB):
                pe.wait_ge(cy_sq, i + 1)
                last = mm(o[:, :], C(C_M512), glu[:, i, 0:T], i == 0, i == CB - 1)
            last.then_inc(filled[2], 1)
            for i, b in enumerate(GROUP_BANKS):
                o = begin(f"gvar{i}", b)
                pe.wait_ge(ysq_ready, i + 1)
                mm(o[:, :], C(C_HEADM), gsq[:, i, :]).then_inc(filled[b], 1)
            pe.wait_ge(hl_again, DC)
            mix_block(0)
            mix_block(1)
            for i, b in enumerate((2, 7)):
                o = begin(f"gate{i}", b)
                mm(o[:, :], g2_s[:, i * P:(i + 1) * P], lgs[:, :]).then_inc(filled[b], 1)
            mix_block(2)
            mix_block(3)
            for i, b in ((2, 2), (3, 7)):
                o = begin(f"gate{i}", b)
                mm(o[:, :], g2_s[:, i * P:(i + 1) * P], lgs[:, :]).then_inc(filled[b], 1)

            for k in range(4, len(MIX_ORDER)):
                mix_block(k)
            pe.wait_ge(mix_ready, 2 * DC)
            for d in range(DC):
                project(f"wout{d}", 3 + d % 2, W_OUT + d, mixH, mixL)

            mean_square("ms2", 7, rs2, 1)


            def key_scores(m):
                o = begin(f"sc{m}", 1 + m % 2)
                wait_taken(pe, f"q{m}")
                pe.wait_ge(s_keys, 16)
                for t in range(TT):
                    last = mm(o[:, t * P:(t + 1) * P], qt[:, m % 2, t * P:(t + 1) * P], keys[:, m, :])
                last.then_inc(fill_sem(f"sc{m}"), 1)

            for m in range(2 * PKH):
                project(f"q{m}", 3 + m % 2, W_Q + m, h2H, h2L, None if m else DC)
                if m:
                    key_scores(m - 1)
            key_scores(2 * PKH - 1)

            def scores(n, s, quarter=None):
                if not quarter:
                    pe.wait_ge(ul_ready, n + 1)
                    pe.wait_ge(gelu_ready, n + 1)
                for c in range(DC) if quarter is None else (2 * quarter, 2 * quarter + 1):
                    last = mm3(bank[4 + s][:, :], uH[:, s, c, :], uL[:, s, c, :], h2H[:, c, :], h2L[:, c, :],
                               c == 0, c == DC - 1)
                if c == DC - 1:
                    last.then_inc(scores_done, 1)

            for b in (4, 5):
                pe.wait_ge(taken[b], takes[b])
            with pe.Fori(0, NPRE // 8) as i:
                for j in range(4):
                    scores(4 * i + j, j % 2)

            pe.wait_ge(ee_ready, 1)
            for t in range(TT):
                for j, (name, src) in enumerate((("e1", ee[:, t, 0, :]), ("e2", ee[:, t, 1, :]),
                                                 ("gt", best[:, t].rearrange("p a b -> p (a b)")))):
                    o = begin(f"{name}T{t}", j)
                    pe.transpose(o[:, 0:P], src, C(C_ID)).then_inc(fill_sem(f"{name}T{t}"), 1)

            for b in range(8):
                pe.wait_ge(taken[b], takes[b])
            pe.sem_inc(wmm_done, 4)
            with pe.Fori(0, NPRE // 8) as i:
                for j in range(4):
                    for b in range(4):
                        batch = 16 * i + 4 * j + b
                        pe.wait_ge(oh2_ready, batch + 1)
                        pe.wait_ge(rh_ready, batch + 1)
                        pe.wait_ge(wst_ready, batch + 1)
                        o = bank[6 + b % 2]
                        for k in range(4):
                            last = mm(o[:, k * P:(k + 1) * P], oh2[:, b, k, :], rh[:, b, k, :])
                        last.then_inc(wmm_done, 1)
                        scores(NPRE // 2 + 4 * i + j, j % 2, b)

            def unit(q, par, u):
                g, sweep = u % G, u // G
                pe.wait_ge(al_ready, G * q + g + 1)
                pe.wait_ge(vl_ready, 2 * G * q + u + 1)
                slot = par * G + g
                for j in range(4):
                    if g == 0:
                        pe.wait_ge(acc_added, 8 * q + 4 * sweep + j + 1)
                    last = mm3(bank[j][:, :], vH[:, u % 4, j * P:(j + 1) * P], vL[:, u % 4, j * P:(j + 1) * P],
                               aH[:, slot, :], aL[:, slot, :], g == 0, g == G - 1)
                    if g == G - 1:
                        last.then_inc(sweep_done, 1)
                    elif j == 3:
                        last.then_inc(unit_done, 1)

            def group(q, par, more):
                for sweep in range(2):
                    for g in range(G):
                        unit(q, par, G * sweep + g)
                    if more:
                        scores(NPRE + 2 * (q + 1) + sweep, sweep)

            scores(NPRE, 0)
            scores(NPRE + 1, 1)
            with pe.Fori(0, NG // 2 - 1) as i:
                group(2 * i, 0, True)
                group(2 * i + 1, 1, True)
            group(NG - 2, 0, True)
            group(NG - 1, 1, False)

            mean_square("ms3", 7, rs3, 2)

        @block.sync
        def _(sp):
            for i in range(2):
                half = slice(i * DC // 2, (i + 1) * DC // 2)
                sp.dma_start(xin[:, half, :], xT[:, half, :]).then_inc(s_x[i], 16)
            sp.dma_start(cst[:, :, :], consts).then_inc(s_cst, 16)
            sp.dma_start(rst[:, :], reset).then_inc(s_cst, 16)
            sp.dma_start(vec[:, :], vecs).then_inc(s_cst, 16)
            sp.dma_start(wlo[:, :, :], wlora).then_inc(s_lora, 16)
            for s in range(WRAW):
                sp.dma_start(wraw[:, s, :, :], wall[s]).then_inc(w_loaded[s], 16)
            sp.dma_start(w2a2_s[:, :], w2a2).then_inc(s_small, 16)
            sp.dma_start(g2_s[:, :], g2).then_inc(s_small, 16)
            with sp.Fori(1, NW // WRAW) as i:
                for s in range(WRAW):
                    sp.wait_ge(wl_ready, WRAW * i + s - WRAW + 1)
                    sp.dma_start(wraw[:, s, :, :], wall[bass.ds(WRAW * i + s, 1)].rearrange(
                        "o p c n -> p (o c) n")).then_inc(w_loaded[s], 16)

            def load_u(row, slot):
                src = uT[row] if isinstance(row, int) else uT[bass.ds(row, 1)].rearrange("o p c n -> p (o c) n")
                sp.dma_start(uraw[:, slot, :, :], src).then_inc(u_loaded[slot], 16)

            def pre_row(i, j):
                return 2 * G * i + G * (j // 2) + j % 2

            def load_v(q, u):
                g, half = u % G, u // G
                sp.dma_start(vraw[:, half, g, :], v_tab[bass.ds((G * q + g) * P, P), half * 512:(half + 1) * 512]
                             ).then_inc(v_loaded[u], 16)

            def load_wg(q, par):
                sp.dma_start(wg[:, par], w_dram[:, :, bass.ds(q * G, G), :].rearrange("b p e t -> p b e t")
                             ).then_inc(wg_loaded[par], 16)
                sp.dma_start(gl[:, par], g_dram[bass.ds(q * PRE, PRE)].rearrange("n p t -> p n t")
                             ).then_inc(wg_loaded[par], 16)

            def store_g(n, s):
                sp.wait_ge(gelu_ready, n + 3)
                dst = g_dram[n] if isinstance(n, int) else g_dram[bass.ds(n, 1)].rearrange("n p t -> p (n t)")
                sp.dma_start(dst, ge[:, s, :]).then_inc(g_stored[s], 16)

            sp.wait_ge(wl_ready, NW)
            for j in range(4):
                load_u(pre_row(0, j), j)
            with sp.Fori(0, NPRE // 8) as i:
                for j in range(4):
                    sp.wait_ge(ul_ready, 4 * i + j + 1)
                    load_u(pre_row(i + 1, j), j)
                    store_g(4 * i + j, j % 2)
            sp.wait_ge(ee_ready, 1)
            for u in range(2 * G):
                load_v(0, u)

            def beside_w(i, last):
                for j in range(4):
                    n = NPRE // 2 + 4 * i + j
                    sp.wait_ge(ul_ready, n + 1)
                    load_u(G * (j // 2) + PRE + j % 2 if last else pre_row(NPRE // 8 + i + 1, j), j)
                    if j % 2:
                        sp.wait_ge(wst_ready, 2 + 16 * i + 8 * (j // 2) + 8)
                        b = j // 2
                        sp.dma_start(w_dram[bass.ds(2 * i + b, 1)].rearrange("b p e t -> p (b e) t"),
                                     wst[:, b, :, :]).then_inc(wst_stored[b], 16)
                    store_g(n, j % 2)

            with sp.Fori(0, NPRE // 8 - 1) as i:
                beside_w(i, False)
            beside_w(NPRE // 8 - 1, True)
            for i in range(2):
                sp.wait_ge(wst_stored[i], 16 * NTB // 2)
                sp.wait_ge(g_stored[i], 16 * NPRE // 2)
            load_wg(0, 0)
            load_wg(1, 1)

            def group_loads(q, par, more):
                for s in range(2):
                    if more:
                        sp.wait_ge(ul_ready, NPRE + 2 * q + s + 1)
                        load_u(G * (q + 2) + PRE + s, 2 * par + s)
                    for u in range(4 * s, 4 * s + 4):
                        sp.wait_ge(vl_ready, 2 * G * q + u + 1)
                        load_v(q + 1, u)
                    if s == 0 and more:
                        sp.wait_ge(act_ready, G * q + G)
                        load_wg(q + 2, par)

            with sp.Fori(0, NG // 2 - 1) as i:
                group_loads(2 * i, 0, True)
                group_loads(2 * i + 1, 1, True)
            group_loads(NG - 2, 0, False)
            for c in range(DC):
                sp.wait_ge(y_ready, c + 1)
                sp.dma_start(yT[c], x1[:, c, :]).then_inc(y_stored[c % 2], 16)
            for i in range(2):
                sp.wait_ge(y_stored[i], 16 * DC // 2)

        @block.scalar
        def _(act):
            def fn(out, in_, f, **kw):
                return act.activation(out, in_, f, **kw)

            def root(out, name, k):
                return fn(out, ps(name)[:, :], ACT.Sqrt, bias=vc("eps", k))

            def wjob(n):
                if n < W_MIX:
                    return f"w{n}"
                if n < W_OUT:
                    kind, d = MIX_ORDER[n - W_MIX]
                    return {"a": "ga", "b": "gb", "p": "wo"}[kind] + str(d)
                return f"wout{n - W_OUT}" if n < W_Q else f"q{n - W_Q}"

            def split_h(n):
                if n >= NW:
                    return
                act.wait_ge(w_loaded[n % WRAW], 16 * (n // WRAW + 1))
                if n >= WSPL:
                    wait_filled(act, wjob(n - WSPL))
                fn(wH[:, n % WSPL, :, :], wraw[:, n % WRAW, :, :], ACT.Copy).then_inc(wh_ready, 1)

            for c in range(DC):
                if c % (DC // 2) == 0:
                    act.wait_ge(s_x[c // (DC // 2)], 16)
                if c >= 2:
                    act.wait_ge(sum_grown, c - 1)
                fn(sq[:, c % 2, :], xin[:, c, :], ACT.Square).then_inc(sq_ready, 1)
            act.wait_ge(s_lora, 16)
            fn(wloH[:, :, :], wlo[:, :, :], ACT.Copy).then_inc(wloh_ready, 1)
            wait_filled(act, "ms1")
            act.wait_ge(s_cst, 48)
            root(rs[:, :], "ms1", 0).then_inc(take_sem("ms1"), 1)
            split_h(0)
            split_h(1)
            for c in range(DC):
                act.wait_ge(h_new, c + 1)
                fn(hH[:, c, :], h[:, c, :], ACT.Copy).then_inc(h_high, 1)
            act.wait_ge(zero_ready, 1)
            slot = 0
            for name, n in (("lora_a", LW + LA), ("lora_b", LG)):
                wait_filled(act, name)
                fn(shift[0:n, slot, 1:], ps(name)[0:n, :], ACT.Copy).then_inc(take_sem(name), 1)
                slot += 1
            act.wait_ge(lora_shifted, 1)
            fn(lwa[0:LW, :], sgb[0:LW, :], ACT.Tanh).then_inc(lora_ready, 1)
            act.wait_ge(lora_shifted, 2)
            fn(lgs[:, :], sgb[0:LG, :], ACT.Sigmoid).then_inc(lora_ready, 1)
            for n in range(12):
                wait_filled(act, f"w{n}")
                if n >= 2:
                    act.wait_ge(rkv_ready, n - 1)
                else:
                    act.wait_ge(lora_shifted, 2)
                fn(shift[:, n % 2, 1:], ps(f"w{n}")[:, :], ACT.Copy).then_inc(take_sem(f"w{n}"), 1)
                split_h(n + 2)
            def conv_squares():
                for i in range(CB):
                    if i < CB - 1:
                        act.wait_ge(cy_norm, i + 1)
                    else:
                        wait_taken(act, "cmean")
                    fn(glu[:, i, 0:T], cy[:, i, :], ACT.Square).then_inc(cy_sq, 1)

            def decay_and_a(t):
                for name, dst, col in (("zw", ld, "w0"), ("za", aa, "a0")):
                    wait_filled(act, f"{name}{t}")
                    if t:
                        act.wait_ge(feats_ready, t)
                    for i in range(CB):
                        last = fn(dst[:, i, :], ps(f"{name}{t}")[:, i * P:(i + 1) * P], ACT.Sigmoid,
                                  bias=vc(col, i))
                    last.then_inc(take_sem(f"{name}{t}"), 1)

            def kk_squares(t):
                act.wait_ge(kn_ready, t + 1)
                if t:
                    wait_filled(act, f"rk{t - 1}")
                fn(sqh[:, :, :], kn[:, :, :], ACT.Square).then_inc(sqk_ready, 1)

            def kk_root(t):
                wait_taken(act, f"kn{t}")
                fn(be[:, t % 2], be[:, t % 2], ACT.Sqrt).then_inc(kn_root, 1)

            def exps(t):
                act.wait_ge(cum_ready, t + 1)
                fn(em[:, :, :], bb[:, :, :], ACT.Exp, scale=-1.0)
                fn(ep[:, :, :], bb[:, :, :], ACT.Exp)
                fn(ex[:, :, :], ex[:, :, :], ACT.Exp).then_inc(exps_ready, 1)

            def token_copies(t):
                for name, dst in (("nkt", nkt_tok), ("v", v_tok), ("be", be_tok), ("ke", ke_tok)):
                    wait_filled(act, f"{name}T{t}")
                    if t >= 2:
                        wait_filled(act, f"Y{2 * t - 3}")
                    fn(dst[:, t % 2, :], ps(f"{name}T{t}")[:, :], ACT.Copy).then_inc(take_sem(f"{name}T{t}"), 1)

            def chunk_copies(c):
                rows = slice(CHUNK * (c % 2), CHUNK * (c % 2) + CHUNK)
                wait_filled(act, f"SA{c}")
                if c:
                    wait_filled(act, f"Y{c - 1}")
                fn(sa[rows, :], ps(f"SA{c}")[rows, :], ACT.Copy).then_inc(take_sem(f"SA{c}"), 1)
                wait_filled(act, f"Y{c}")
                fn(yt[:, :, c * CHUNK:(c + 1) * CHUNK],
                   ps(f"Y{c}")[:, 0:CB * CHUNK].rearrange("p (a b) -> p a b", b=CHUNK), ACT.Copy).then_inc(
                       take_sem(f"Y{c}"), 1)

            for i in range(CB):
                n = W_CONV + 2 * i
                wait_filled(act, f"w{n}")
                if i:
                    wait_taken(act, f"w{n - 1}")
                fn(sgb[:, :], ps(f"w{n}")[:, :], ACT.Sigmoid).then_inc(take_sem(f"w{n}"), 1)
                if n + 3 < W_MIX:
                    split_h(n + 2)
                    split_h(n + 3)
                if i == 0:
                    decay_and_a(0)
                    kk_squares(0)
                elif i == 1:
                    kk_root(0)
                    exps(0)
            token_copies(0)
            for t in range(TT):
                more = t + 1 < TT
                if more:
                    decay_and_a(t + 1)
                wait_filled(act, f"W1{t}")
                if t:
                    wait_filled(act, f"Y{2 * t - 1}")
                fn(w1t[:, :, :], ps(f"W1{t}")[:, :].rearrange("p (a b) -> p a b", b=P), ACT.Copy).then_inc(
                    take_sem(f"W1{t}"), 1)
                wait_filled(act, f"MV{t}")
                fn(mv[:, :], ps(f"MV{t}")[:, :], ACT.Copy).then_inc(take_sem(f"MV{t}"), 1)
                if more:
                    kk_squares(t + 1)
                    kk_root(t + 1)
                chunk_copies(2 * t)
                if more:
                    exps(t + 1)
                chunk_copies(2 * t + 1)
                if more:
                    token_copies(t + 1)

            split_h(W_MIX)
            split_h(W_MIX + 1)
            for c in range(DC):
                fn(hH[:, c, :], h[:, c, :], ACT.Copy).then_inc(h_again, 1)
            conv_squares()
            for i in range(CB):
                wait_taken(act, f"gmean{i}")
                fn(gsq[:, i, :], yt[:, i, :], ACT.Square).then_inc(ysq_ready, 1)

            def gate(k):
                kind, d = MIX_ORDER[k]
                name = f"g{kind}{d}"
                wait_filled(act, name)
                if d >= 2:
                    act.wait_ge(mix_ready, 2 * (d - 1))
                fn((sga if kind == "a" else sgw)[:, d % 2, :], ps(name)[:, :], ACT.Sigmoid).then_inc(
                    take_sem(name), 1)
                split_h(W_MIX + k + 2)

            wait_filled(act, "cvar")
            root(cdev[:, :], "cvar", 1).then_inc(take_sem("cvar"), 1)
            for i in range(CB):
                wait_filled(act, f"gvar{i}")
                root(gdev[:, i, :], f"gvar{i}", 2).then_inc(take_sem(f"gvar{i}"), 1)
            gate(0)
            gate(1)
            for i in range(CB):
                act.wait_ge(cy_norm, CB - 1 + i + 1)
                fn(glu[:, i, 0:T], cy[:, i, :], ACT.Sigmoid).then_inc(cy_sig, 1)
            for i in range(CB):
                if i in (1, 3):
                    gate(2 + i // 2)
                wait_taken(act, f"gate{i}")
                fn(oH[:, i, :], yt[:, i, :], ACT.Copy).then_inc(o_high, 1)

            for k in range(4, len(MIX_ORDER)):
                if MIX_ORDER[k][0] == "p":
                    wait_filled(act, f"wo{MIX_ORDER[k][1]}")
                    split_h(W_MIX + k + 2)
                else:
                    gate(k)
            for d in range(DC):
                wait_filled(act, f"wout{d}")
                split_h(W_OUT + d + 2)
                wait_taken(act, f"wout{d}")
                if d >= 2:
                    act.wait_ge(sum_grown, DC + d - 1)
                fn(sq2[:, d % 2, :], x1[:, d, :], ACT.Square).then_inc(sq_ready, 1)
            wait_filled(act, "ms2")
            root(rs2[:, :], "ms2", 0).then_inc(take_sem("ms2"), 1)
            for c in range(DC):
                act.wait_ge(h_new, DC + c + 1)
                fn(h2H[:, c, :], h2f[:, c % 2, :], ACT.Copy).then_inc(h_high, 1)
            for m in range(2 * PKH):
                wait_filled(act, f"q{m}")
                if m >= 2:
                    wait_filled(act, f"sc{m - 2}")
                fn(qt[:, m % 2, :], ps(f"q{m}")[:, :], ACT.Copy).then_inc(take_sem(f"q{m}"), 1)
                split_h(W_Q + m + 2)
            def u_high(n, lap, slot):
                act.wait_ge(u_loaded[slot], 16 * lap + 16)
                if not (isinstance(n, int) and n < 2):
                    act.wait_ge(scores_done, n - 1)
                fn(uH[:, slot % 2, :, :], uraw[:, slot, :, :], ACT.Copy).then_inc(uh_ready, 1)

            def gelu(n, s):
                act.wait_ge(scores_done, n + 1)
                fn(ge[:, s, :], bank[4 + s][:, :], ACT.Gelu).then_inc(gelu_ready, 1)

            def ahead(n0, i, j):
                u_high(n0 + 4 * i + j + 1, n0 // 4 + i + (j + 1) // 4, (j + 1) % 4)

            act.sem_inc(gelu_ready, 2)
            u_high(0, 0, 0)
            for j in range(2):
                ahead(0, 0, j)
                gelu(j, j)
            for j in (2, 3):
                ahead(0, 0, j)
                act.wait_ge(g_stored[j % 2], 16)
                gelu(j, j % 2)
            with act.Fori(1, NPRE // 8) as i:
                for j in range(4):
                    ahead(0, i, j)
                    act.wait_ge(g_stored[j % 2], 16 * (2 * i + j // 2))
                    gelu(4 * i + j, j % 2)
            act.wait_ge(best_sub, 1)
            fn(best[:, :, :, :], best[:, :, :, :], ACT.Exp).then_inc(best_exp, 1)
            for t in range(TT):
                for j, name in enumerate(("e1", "e2", "gt")):
                    wait_filled(act, f"{name}T{t}")
                    fn(et[:, j, t * P:(t + 1) * P], ps(f"{name}T{t}")[:, 0:P], ACT.Copy).then_inc(
                        take_sem(f"{name}T{t}"), 1)
            act.sem_inc(wst_ready, 2)

            def w_batches(i, j):
                for b in range(4):
                    act.wait_ge(wmm_done, 4 + 16 * i + 4 * j + b + 1)
                    o = 4 * (4 * (j % 2) + b)
                    fn(wst[:, j // 2, :, o:o + 4].rearrange("p e t -> p t e"),
                       bank[6 + b % 2][:, :].rearrange("p (t e) -> p t e", t=4), ACT.Copy).then_inc(wst_ready, 1)

            def beside_w(i, first):
                for j in range(4):
                    if not first and j % 2 == 0:
                        act.wait_ge(wst_stored[j // 2], 16 * i)
                    w_batches(i, j)
                    ahead(NPRE // 2, i, j + 1)
                    act.wait_ge(g_stored[j % 2], 16 * (NPRE // 4 + 2 * i + j // 2))
                    gelu(NPRE // 2 + 4 * i + j, j % 2)

            ahead(NPRE // 2, 0, 0)
            beside_w(0, True)
            with act.Fori(1, NPRE // 8) as i:
                beside_w(i, False)

            def a_high(q, par, g):
                act.wait_ge(act_ready, G * q + g + 1)
                fn(aH[:, par * G + g, :], af[:, g % 2, :], ACT.Copy).then_inc(ah_ready, 1)

            def v_high(q, u):
                act.wait_ge(v_loaded[u], 16 * q + 16)
                if not (isinstance(q, int) and q == 0 and u < 4):
                    prev_q, pu = (q, u - 4) if u >= 4 else (q - 1, u + 4)
                    if pu % G == G - 1:
                        act.wait_ge(sweep_done, 8 * prev_q + 4 * (pu // G) + 4)
                    else:
                        act.wait_ge(unit_done, 6 * prev_q + 3 * (pu // G) + pu % G + 1)
                fn(vH[:, u % 4, :], vraw[:, u // G, u % G, :], ACT.Copy).then_inc(vh_ready, 1)

            def own_gelu(q, s):
                if isinstance(q, int) and q == 0:
                    act.wait_ge(g_stored[s], 16 * NPRE // 2)
                else:
                    act.wait_ge(act_ready, G * (q - 1) + PRE + s + 1)
                gelu(NPRE + 2 * q + s, s)

            own_gelu(0, 0)
            for g in range(G - 1):
                a_high(0, 0, g)
            for u in range(4):
                v_high(0, u)

            def step(i, par, more):
                q = 2 * i + par
                own_gelu(q, 1)
                a_high(q, par, G - 1)
                lap, base = NPRE // 4 + i + par, 2 * (1 - par)
                if more:
                    u_high(NPRE + 2 * (q + 1), lap, base)
                for u in range(4, 8):
                    v_high(q, u)
                if more:
                    a_high(q + 1, 1 - par, 0)
                    a_high(q + 1, 1 - par, 1)
                    u_high(NPRE + 2 * (q + 1) + 1, lap, base + 1)
                    own_gelu(q + 1, 0)
                    a_high(q + 1, 1 - par, 2)
                    for u in range(4):
                        v_high(q + 1, u)

            with act.Fori(0, NG // 2 - 1) as i:
                step(i, 0, True)
                step(i, 1, True)
            step(NG // 2 - 1, 0, True)
            step(NG // 2 - 1, 1, False)

            for c in range(DC):
                act.wait_ge(acc_added, 4 + 8 * (NG - 1) + (4 if c < 4 else c + 1))
                if c >= 2:
                    act.wait_ge(sum_grown, 2 * DC + c - 1)
                fn(sq3[:, c % 2, :], x1[:, c, :], ACT.Square).then_inc(sq_ready, 1)
            wait_filled(act, "ms3")
            root(rs3[:, :], "ms3", 0).then_inc(take_sem("ms3"), 1)

        @block.vector
        def _(dve):
            count = [0]

            def tick(ins):
                count[0] += 1
                ins.then_inc(dve_order, 1)

            def after():
                dve.wait_ge(dve_order, count[0])

            tt, tsc, stt = dve.tensor_tensor, dve.tensor_scalar, dve.scalar_tensor_tensor

            def split_l(n):
                if n >= NW:
                    return
                dve.wait_ge(wh_ready, n + 1)
                tt(wL[:, n % WSPL, :, :], wraw[:, n % WRAW, :, :], wH[:, n % WSPL, :, :], ALU.subtract).then_inc(
                    wl_ready, 1)

            tick(dve.memset(shift[:, :, 0:1], 0.0))
            dve.memset(glu[:, :, 0:TAPS - 1], 0.0).then_inc(zero_ready, 1)
            def grow_sum(nth, total, sqt, c):
                dve.wait_ge(sq_ready, nth * DC + c + 1)
                if c:
                    dve.wait_ge(sum_grown, nth * DC + c)
                    tt(total[:, :], total[:, :], sqt[:, c % 2, :], ALU.add).then_inc(sum_grown, 1)
                else:
                    dve.tensor_copy(total[:, :], sqt[:, 0, :]).then_inc(sum_grown, 1)

            for c in range(DC):
                grow_sum(0, rs, sq, c)
            dve.wait_ge(s_cst, 48)
            tick(tsc(omka[:, :], vc("ka", 0, CB), -1.0, 1.0, ALU.mult, ALU.add))
            dve.wait_ge(wloh_ready, 1)
            tt(wloL[:, :, :], wlo[:, :, :], wloH[:, :, :], ALU.subtract).then_inc(wlol_ready, 1)
            wait_taken(dve, "ms1")
            tick(dve.reciprocal(rs[:, :], rs[:, :]))
            after()
            for c in range(DC + 1):
                if c < DC:
                    stt(h[:, c, :], xin[:, c, :], vc("gmix", c), rs[:, :], ALU.mult, ALU.mult).then_inc(h_new, 1)
                if c:
                    dve.wait_ge(h_high, c)
                    tt(hL[:, c - 1, :], h[:, c - 1, :], hH[:, c - 1, :], ALU.subtract).then_inc(h_split, 1)

            split_l(0)
            split_l(1)
            wait_taken(dve, "lora_a")
            tick(tt(sdiff[0:64, :], shift[0:64, 0, 0:T], shift[0:64, 0, 1:], ALU.subtract))
            after()
            stt(sgb[0:64, :], sdiff[0:64, :], vc("mua", 0, 1, 64), shift[0:64, 0, 1:], ALU.mult, ALU.add).then_inc(
                lora_shifted, 1)
            dve.wait_ge(lora_shifted, 1)
            tick(dve.tensor_copy(lwa[32:64, :], sgb[32:64, :]))
            dve.wait_ge(lora_ready, 1)
            wait_taken(dve, "lora_b")
            tick(tt(sdiff[0:LG, :], shift[0:LG, 1, 0:T], shift[0:LG, 1, 1:], ALU.subtract))
            after()
            stt(sgb[0:LG, :], sdiff[0:LG, :], vc("mub", 0, 1, LG), shift[0:LG, 1, 1:], ALU.mult, ALU.add).then_inc(
                lora_shifted, 1)
            for n in range(12):
                dst = (r_in, k_in, v_in)[n // 4]
                wait_taken(dve, f"w{n}")
                tick(tt(sdiff[:, :], shift[:, n % 2, 0:T], shift[:, n % 2, 1:], ALU.subtract))
                after()
                stt(dst[:, n % 4, :], sdiff[:, :], vc("mu", n), shift[:, n % 2, 1:], ALU.mult, ALU.add).then_inc(
                    rkv_ready, 1)
                dve.wait_ge(rkv_ready, n + 1)
                split_l(n + 2)
            done_taps, last_tap = [0], [0]

            def taps(k):
                for _ in range(k):
                    i, j = CB - 1, done_taps[0]
                    if j == TAPS:
                        return
                    done_taps[0] += 1
                    if j == 0:
                        ins = tsc(cy[:, i, :], glu[:, i, 0:T], vc("dw", i * TAPS), vc("dwb", i), ALU.mult, ALU.add)
                    else:
                        dve.wait_ge(dve_order, last_tap[0])
                        ins = stt(cy[:, i, :], glu[:, i, j:j + T], vc("dw", i * TAPS + j), cy[:, i, :],
                                  ALU.mult, ALU.add)
                    if j < TAPS - 1:
                        tick(ins)
                        last_tap[0] = count[0]
                    else:
                        ins.then_inc(conv_last, 1)


            def flat(a):
                return a.rearrange("p a b -> p (a b)")

            def masked(name, dst, mask, par):
                wait_filled(dve, name)
                m = C(mask).unsqueeze(1).broadcast_to([P, 4, P])
                tt(dst, ps(name)[:, :].rearrange("p (a b) -> p a b", b=P), m, ALU.mult).then_inc(take_sem(name), 1)

            def decays(t):
                tsl, s = slice(t * P, (t + 1) * P), t % 2
                wait_taken(dve, f"zw{t}")
                tick(tsc(flat(ld[:, :, :]), flat(ld[:, :, :]), -float(np.exp(-0.5)), None, ALU.mult))
                after()
                if t >= 2:
                    wait_filled(dve, f"Y{2 * t - 3}")
                tick(dve.tensor_tensor_scan(flat(bb[:, :, :]), rst[:, :], flat(ld[:, :, :]), 0.0, ALU.mult, ALU.add))
                after()
                tt(flat(ex[:, :, :]), flat(bb[:, :, :]), flat(ld[:, :, :]), ALU.subtract).then_inc(cum_ready, 1)
                tt(kn[:, :, :], k_in[:, :, tsl], bc(vc("kk", 0, CB), P), ALU.mult).then_inc(kn_ready, 1)
                wait_taken(dve, f"za{t}")
                for i in range(CB):
                    ins = tsc(k2[:, i, :], aa[:, i, :], vc("ka", i), omka[:, i:i + 1], ALU.mult, ALU.add)
                tick(ins)
                after()
                tick(tt(k2[:, :, :], k_in[:, :, tsl], k2[:, :, :], ALU.mult))
                wait_filled(dve, f"kn{t}")
                tsc(flat(be[:, s]), ps(f"kn{t}")[:, :], 1e-24, None, ALU.max).then_inc(take_sem(f"kn{t}"), 1)
                after()

            def keys(t):
                tsl, s = slice(t * P, (t + 1) * P), t % 2
                for i in range(CB):
                    ins = stt(sqh[:, i, :], r_in[:, i, tsl], vc("rk", i), k2[:, i, :], ALU.mult, ALU.mult)
                ins.then_inc(rk_ready, 1)
                dve.wait_ge(kn_root, t + 1)
                tick(dve.reciprocal(flat(be[:, s]), flat(be[:, s])))
                after()
                dve.wait_ge(kn_ready, t + 1)
                tick(stt(flat(kn[:, :, :]), flat(kn[:, :, :]), -1.0, flat(be[:, s]), ALU.mult, ALU.mult))
                after()

            def rates(t):
                tsl, s = slice(t * P, (t + 1) * P), t % 2
                dve.wait_ge(exps_ready, t + 1)
                tick(stt(flat(bb[:, :, :]), flat(kn[:, :, :]), -1.0, flat(aa[:, :, :]), ALU.mult, ALU.mult))
                tt(nkt[:, s], kn[:, :, :], ex[:, :, :], ALU.mult)
                tt(rt[:, s], r_in[:, :, tsl], ep[:, :, :], ALU.mult)

            def scaled(t):
                tsl, s = slice(t * P, (t + 1) * P), t % 2
                tick(tt(kh[:, s], k2[:, :, :], em[:, :, :], ALU.mult))
                tick(dve.tensor_copy(pend[:, s], ep[:, :, CHUNK - 1::CHUNK]))
                after()
                tick(tt(bh[:, s], bb[:, :, :], em[:, :, :], ALU.mult))
                wait_filled(dve, f"rk{t}")
                tt(bonus[:, :, tsl], ps(f"rk{t}")[:, :].rearrange("p (a b) -> p a b", b=P), v_in[:, :, tsl],
                   ALU.mult).then_inc(take_sem(f"rk{t}"), 1)
                after()
                for src, dst in ((bh, be), (kh, ke)):
                    for i in range(CB):
                        pe_ = pend[:, s, i, :].unsqueeze(2).broadcast_to([P, 2, CHUNK])
                        ins = tt(dst[:, s, i, :].rearrange("p (c n) -> p c n", n=CHUNK),
                                 src[:, s, i, :].rearrange("p (c n) -> p c n", n=CHUNK), pe_, ALU.mult)
                ins.then_inc(feats_ready, 1)

            def masks_and_inverse(t):
                s = t % 2
                ident4 = C(C_ID).unsqueeze(1).broadcast_to([P, 4, P])
                for par in range(2):
                    name = f"M{par}_{t}"
                    wait_filled(dve, name)
                    tick(tt(xx[:, par], ps(name)[:, :].rearrange("p (a b) -> p a b", b=P),
                            C(C_E1).unsqueeze(1).broadcast_to([P, 4, P]), ALU.mult))
                    after()
                    tt(nn[:, par], xx[:, par], ident4, ALU.add).then_inc(take_sem(name), 1)
                for par in range(2):
                    name = f"MT{par}_{t}"
                    wait_filled(dve, name)
                    tick(tt(lt[:, par], ps(name)[:, :].rearrange("p (a b) -> p a b", b=P),
                            C(C_STRICT).unsqueeze(1).broadcast_to([P, 4, P]), ALU.mult))
                    after()
                    tick(tt(nt[:, s, par], lt[:, par], C(C_E1T).unsqueeze(1).broadcast_to([P, 4, P]), ALU.mult))
                    after()
                    tt(nt[:, s, par], nt[:, s, par], ident4, ALU.add).then_inc(take_sem(name), 1)
                for name, dst, mask in (("ak", mak, C_STRICT), ("rb", mrb, C_INCL), ("rq", mrk, C_INCL)):
                    for par in range(2):
                        masked(f"{name}{par}_{t}", dst[:, par] if dst is mak else dst[:, s, par], mask, par)
                for lv in range(5):
                    for par in range(2):
                        masked(f"X{lv}{par}_{t}", xx[:, par], (C_E2, C_E4, C_E8, C_E16, C_E32)[lv], par)
                    for par in range(2):
                        for name, dst in ((f"N{lv}{par}_{t}", nn[:, par]), (f"NT{lv}{par}_{t}", nt[:, s, par])):
                            if name not in turn:
                                continue
                            wait_filled(dve, name)
                            tt(dst, ps(name)[:, :].rearrange("p (a b) -> p a b", b=P), dst, ALU.add).then_inc(
                                take_sem(name), 1)

            def decayed_state(c):
                s = (c // 2) % 2
                if c:
                    wait_taken(dve, f"ST{c - 1}")
                else:
                    dve.wait_ge(state_ready, 1)
                tick(tt(sdec[:, :, :], state[:, :, :], bc(pend[:, s, :, c % 2], P), ALU.mult))

            def new_state(c):
                after()
                wait_filled(dve, f"ST{c}")
                wait_filled(dve, f"SA{c}")
                wait_filled(dve, f"Y{c}")
                for par in range(2):
                    rows = slice(HD * par, HD * par + HD)
                    ins = tt(state[rows, :, rows],
                             ps(f"ST{c}")[rows, :].rearrange("p (a b) -> p a b", b=P)[:, :, rows],
                             sdec[rows, :, rows], ALU.add)
                ins.then_inc(take_sem(f"ST{c}"), 1)

            dve.wait_ge(zero_ready, 1)
            dve.memset(state[:, :, :], 0.0).then_inc(state_ready, 1)
            for i in range(CB):
                n = W_CONV + 2 * i
                if n + 3 < W_MIX:
                    split_l(n + 2)
                wait_taken(dve, f"w{n}")
                wait_filled(dve, f"w{n + 1}")
                tt(glu[:, i, TAPS - 1:], ps(f"w{n + 1}")[:, :], sgb[:, :], ALU.mult).then_inc(take_sem(f"w{n + 1}"), 1)
                if n + 3 < W_MIX:
                    split_l(n + 3)
                if i == 0:
                    decays(0)
                elif i == 1:
                    keys(0)
                    rates(0)
                elif i == 2:
                    scaled(0)
            wait_taken(dve, f"w{W_MIX - 1}")
            for t in range(TT):
                masks_and_inverse(t)
                more = t + 1 < TT
                if more:
                    decays(t + 1)
                decayed_state(2 * t)
                if more:
                    keys(t + 1)
                taps(4)
                new_state(2 * t)
                if more:
                    rates(t + 1)
                decayed_state(2 * t + 1)
                if more:
                    scaled(t + 1)
                taps(4)
                new_state(2 * t + 1)
            taps(TAPS)
            split_l(W_MIX)
            split_l(W_MIX + 1)
            dve.wait_ge(conv_out, CB - 1)
            dve.wait_ge(conv_last, 1)
            wait_filled(dve, "cmean")
            for i in range(CB):
                tt(cy[:, i, :], cy[:, i, :], ps("cmean")[:, :], ALU.subtract).then_inc(
                    cy_norm if i < CB - 1 else take_sem("cmean"), 1)
            for i in range(CB):
                wait_filled(dve, f"gmean{i}")
                tt(yt[:, i, :], yt[:, i, :], ps(f"gmean{i}")[:, :], ALU.subtract).then_inc(take_sem(f"gmean{i}"), 1)
            wait_taken(dve, "cmean")
            wait_taken(dve, "cvar")
            tick(dve.reciprocal(cdev[:, :], cdev[:, :]))
            after()
            for i in range(CB):
                tick(tt(cy[:, i, :], cy[:, i, :], cdev[:, :], ALU.mult))
                after()
                tsc(cy[:, i, :], cy[:, i, :], vc("lng", i), vc("lnb", i), ALU.mult, ALU.add).then_inc(cy_norm, 1)
            def o_low(i):
                dve.wait_ge(o_high, i + 1)
                tt(oL[:, i, :], yt[:, i, :], oH[:, i, :], ALU.subtract).then_inc(o_ready, 1)

            for i in range(CB):
                wait_taken(dve, f"gmean{i}")
                wait_taken(dve, f"gvar{i}")
                tick(dve.reciprocal(gdev[:, i, :], gdev[:, i, :]))
                after()
                split_l(W_MIX + 2 + i)
                tick(stt(yt[:, i, :], yt[:, i, :], vc("gng", i), gdev[:, i, :], ALU.mult, ALU.mult))
                after()
                tick(stt(yt[:, i, :], yt[:, i, :], vc("gnb", i), bonus[:, i, :], ALU.add, ALU.add))
                if i:
                    o_low(i - 1)
                after()
                wait_filled(dve, f"gate{i}")
                tt(yt[:, i, :], yt[:, i, :], ps(f"gate{i}")[:, :], ALU.mult).then_inc(take_sem(f"gate{i}"), 1)
            o_low(CB - 1)
            dve.wait_ge(o_ready, CB)
            for k in range(4, len(MIX_ORDER)):
                kind, d = MIX_ORDER[k]
                if kind != "p":
                    split_l(W_MIX + k + 2)
                    continue
                wait_taken(dve, f"ga{d}")
                wait_filled(dve, f"pw{d}")
                stt(ma[:, :], ps(f"pw{d}")[:, :], vc("pwb", d), sga[:, d % 2, :], ALU.add, ALU.mult).then_inc(
                    take_sem(f"pw{d}"), 1)
                wait_taken(dve, f"gb{d}")
                wait_filled(dve, f"wo{d}")
                tt(mb[:, :], ps(f"wo{d}")[:, :], sgw[:, d % 2, :], ALU.mult).then_inc(take_sem(f"wo{d}"), 1)
                wait_taken(dve, f"pw{d}")
                wait_taken(dve, f"wo{d}")
                tick(tt(mm_[:, :], ma[:, :], mb[:, :], ALU.add))
                after()
                dve.tensor_copy(mixH[:, d, :], mm_[:, :]).then_inc(mix_ready, 1)
                dve.wait_ge(mix_ready, 2 * d + 1)
                tt(mixL[:, d, :], mm_[:, :], mixH[:, d, :], ALU.subtract).then_inc(mix_ready, 1)
                dve.wait_ge(mix_ready, 2 * d + 2)
                split_l(W_MIX + k + 2)
            for d in range(DC):
                dve.wait_ge(xr_loaded, 16)
                wait_filled(dve, f"wout{d}")
                tt(x1[:, d, :], ps(f"wout{d}")[:, :], x1[:, d, :], ALU.add).then_inc(take_sem(f"wout{d}"), 1)
                split_l(W_OUT + d + 2)
                if d:
                    grow_sum(1, rs2, sq2, d - 1)
            grow_sum(1, rs2, sq2, DC - 1)
            wait_taken(dve, "ms2")
            tick(dve.reciprocal(rs2[:, :], rs2[:, :]))
            after()
            for c in range(DC + 1):
                if c < DC:
                    if c >= 2:
                        dve.wait_ge(h_split, DC + c - 1)
                    stt(h2f[:, c % 2, :], x1[:, c, :], vc("gffn", c), rs2[:, :], ALU.mult, ALU.mult).then_inc(h_new, 1)
                if c:
                    dve.wait_ge(h_high, DC + c)
                    tt(h2L[:, c - 1, :], h2f[:, (c - 1) % 2, :], h2H[:, c - 1, :], ALU.subtract).then_inc(h_split, 1)
            for m in range(2 * PKH):
                split_l(W_Q + m + 2)
                hd, half = m // 2, m % 2
                wait_filled(dve, f"sc{m}")
                S = [ps(f"sc{m}")[:, t * P:(t + 1) * P] for t in range(TT)]
                v8 = [tv[:, t, half, hd, 0:8] for t in range(TT)]
                w8 = [tv[:, t, half, hd, 8:16] for t in range(TT)]
                for t in range(TT):
                    tick(dve.max(v8[t], S[t]))
                after()
                for t in range(TT):
                    tick(dve.max_index(ti[:, t, half, hd, 0:8], v8[t], S[t]))
                    ins = dve.match_replace(scr[:, t, :], v8[t], S[t], -3.0e38)
                    if t < TT - 1:
                        tick(ins)
                ins.then_inc(take_sem(f"sc{m}"), 1)
                wait_taken(dve, f"sc{m}")
                for t in range(TT):
                    tick(dve.max(w8[t], scr[:, t, :]))
                after()
                for t in range(TT):
                    tick(dve.max_index(ti[:, t, half, hd, 8:16], w8[t], scr[:, t, :]))
            after()
            iota16 = C(C_IOTA)[:, 0:TOPK]
            for t in range(TT):
                tick(tt(cand[:, :, :, :], bc2(tv[:, t, 0], TOPK), bc1(tv[:, t, 1], TOPK), ALU.add))
                after()
                for hd in range(PKH):
                    cd = cand[:, hd].rearrange("p a b -> p (a b)")
                    tick(dve.max(best[:, t, hd, 0:8], cd))
                    after()
                    tick(dve.max_index(ci[:, t, hd, 0:8], best[:, t, hd, 0:8], cd))
                    tick(dve.match_replace(cscr[:, hd % 2, :], best[:, t, hd, 0:8], cd, -3.0e38))
                    after()
                    tick(dve.max(best[:, t, hd, 8:16], cscr[:, hd % 2, :]))
                    after()
                    tick(dve.max_index(ci[:, t, hd, 8:16], best[:, t, hd, 8:16], cscr[:, hd % 2, :]))
                after()
                cflat = ci[:, t].rearrange("p a b -> p (a b)")
                tick(tsc(c1[:, 0, :], cflat, 4, None, ALU.logical_shift_right))
                tick(tsc(c1[:, 1, :], cflat, TOPK - 1, None, ALU.bitwise_and))
                after()
                tick(dve.tensor_copy(cf[:, :, :], c1[:, :, :]))
                tick(dve.tensor_copy(tif[:, :, :, :], ti[:, t]))
                after()
                for j in range(2):
                    tick(tt(oneh[:, :, :], bc(cf[:, j, :], TOPK),
                            iota16.unsqueeze(1).broadcast_to([P, PKH * TOPK, TOPK]), ALU.is_equal))
                    after()
                    tick(tt(oneh[:, :, :].rearrange("p (h k) n -> p h k n", h=PKH),
                            oneh[:, :, :].rearrange("p (h k) n -> p h k n", h=PKH), bc1(tif[:, j], TOPK), ALU.mult))
                    after()
                    tick(dve.tensor_reduce(ee[:, t, j, :], oneh[:, :, :], AX.X, ALU.add))
                    after()
            hk = "p a b c -> p (a b) c"
            rows = best[:, :, :, :].rearrange(hk)
            tick(dve.tensor_copy(gsum[:, :, :], best[:, :, :, 0]))
            after()
            flat_sum = gsum[:, :, :].rearrange("p a b -> p (a b)")
            tt(rows, rows, bc(flat_sum, TOPK), ALU.subtract).then_inc(best_sub, 1)
            dve.wait_ge(best_exp, 1)
            tick(dve.tensor_reduce(flat_sum, rows, AX.X, ALU.add))
            after()
            tick(dve.reciprocal(flat_sum, flat_sum))
            after()
            tt(rows, rows, bc(flat_sum, TOPK), ALU.mult).then_inc(ee_ready, 1)

            for t in range(TT):
                for n in ("e1", "e2", "gt"):
                    wait_taken(dve, f"{n}T{t}")
            def u_low(n, slot):
                dve.wait_ge(uh_ready, n + 1)
                tt(uL[:, slot % 2, :, :], uraw[:, slot, :, :], uH[:, slot % 2, :, :], ALU.subtract).then_inc(
                    ul_ready, 1)

            dve.wait_ge(ul_ready, NPRE // 2 + 1)
            with dve.Fori(0, NPRE // 8) as i:
                for j in range(4):
                    for b in range(4):
                        dve.wait_ge(wmm_done, 16 * i + 4 * j + b + 1)
                        for k in range(4):
                            tok = bass.ds(2 * T_W * i + 16 * j + 4 * b + k, 1)
                            ins = tsc(rh[:, b, k, :], C(C_IOTA), et[:, 0, tok], et[:, 2, tok],
                                      ALU.is_equal, ALU.mult)
                        tsc(oh2[:, b, 3, :], C(C_IOTA), et[:, 1, tok], None, ALU.is_equal).then_inc(rh_ready, 1)
                        if b == 2:
                            u_low(NPRE // 2 + 4 * i + j + 1, (j + 1) % 4)

            def weigh(q, lap, par, g):
                if g == 0:
                    dve.wait_ge(wg_loaded[par], 32 * lap + 32)
                if g >= PRE:
                    dve.wait_ge(gelu_ready, NPRE + 2 * q + g - PRE + 3)
                if not (isinstance(q, int) and q == 0 and g < 2):
                    dve.wait_ge(al_ready, G * q + g - 1)
                src = gl[:, par, g, :] if g < PRE else ge[:, g - PRE, :]
                tt(af[:, g % 2, :].rearrange("p (b t) -> p b t", t=T_W), src.rearrange("p (b t) -> p b t", t=T_W),
                   wg[:, par, :, g, :], ALU.mult).then_inc(act_ready, 1)

            def a_low(q, par, g):
                dve.wait_ge(ah_ready, G * q + g + 1)
                tt(aL[:, par * G + g, :], af[:, g % 2, :], aH[:, par * G + g, :], ALU.subtract).then_inc(al_ready, 1)

            def v_low(q, u):
                dve.wait_ge(vh_ready, 2 * G * q + u + 1)
                tt(vL[:, u % 4, :], vraw[:, u // G, u % G, :], vH[:, u % 4, :], ALU.subtract).then_inc(vl_ready, 1)

            def add_up(q, sweep):
                for j in range(4):
                    dve.wait_ge(sweep_done, 8 * q + 4 * sweep + j + 1)
                    dst = x1[:, 4 * sweep + j, :]
                    tt(dst, bank[j][:, :], dst, ALU.add).then_inc(acc_added, 1)

            dve.sem_inc(acc_added, 4)
            u_low(NPRE + 1, 1)
            weigh(0, 0, 0, 0)
            weigh(0, 0, 0, 1)
            a_low(0, 0, 0)
            a_low(0, 0, 1)
            weigh(0, 0, 0, 2)
            a_low(0, 0, 2)
            for u in range(4):
                v_low(0, u)

            def step(i, par, more):
                q = 2 * i + par
                base = 2 * (1 - par)
                weigh(q, i, par, G - 1)
                if more:
                    u_low(NPRE + 2 * (q + 1), base)
                a_low(q, par, G - 1)
                for u in (4, 5, 6):
                    v_low(q, u)
                add_up(q, 0)
                v_low(q, 7)
                if not more:
                    for c in range(4):
                        grow_sum(2, rs3, sq3, c)
                if more:
                    nq, nlap, npar = q + 1, i + par, 1 - par
                    weigh(nq, nlap, npar, 0)
                    weigh(nq, nlap, npar, 1)
                    a_low(nq, npar, 0)
                    a_low(nq, npar, 1)
                    u_low(NPRE + 2 * nq + 1, base + 1)
                    weigh(nq, nlap, npar, 2)
                    a_low(nq, npar, 2)
                    for u in (0, 1, 2):
                        v_low(nq, u)
                add_up(q, 1)
                if more:
                    v_low(nq, 3)

            with dve.Fori(0, NG // 2 - 1) as i:
                step(i, 0, True)
                step(i, 1, True)
            step(NG // 2 - 1, 0, True)
            step(NG // 2 - 1, 1, False)

            for c in range(4, DC):
                grow_sum(2, rs3, sq3, c)
            wait_taken(dve, "ms3")
            tick(dve.reciprocal(rs3[:, :], rs3[:, :]))
            after()
            for c in range(DC):
                stt(x1[:, c, :], x1[:, c, :], vc("gf", c), rs3[:, :], ALU.mult, ALU.mult).then_inc(y_ready, 1)

        @block.gpsimd
        def _(pool):
            pool.wait_ge(s_cst, 48)
            pool.wait_ge(zero_ready, 1)
            steps = 0
            for i in range(CB - 1):
                wait_taken(pool, f"w{W_CONV + 2 * i + 1}")
                for j in range(TAPS):
                    if j == 0:
                        ins = pool.tensor_scalar(cy[:, i, :], glu[:, i, 0:T], vc("dw", i * TAPS), vc("dwb", i),
                                                 ALU.mult, ALU.add)
                    else:
                        ins = pool.tensor_tensor(tapped[:, j % 2, :], glu[:, i, j:j + T],
                                                 vc("dw", i * TAPS + j).broadcast_to([P, T]), ALU.mult)
                    ins.then_inc(pool_order, 1)
                    steps += 1
                    if j:
                        pool.wait_ge(pool_order, steps)
                        ins = pool.tensor_tensor(cy[:, i, :], cy[:, i, :], tapped[:, j % 2, :], ALU.add)
                        ins.then_inc(pool_order if j < TAPS - 1 else conv_out, 1)
                        steps += j < TAPS - 1
            for c in range(DC):
                pool.wait_ge(h_again, c + 1)
                pool.tensor_tensor(hL[:, c, :], h[:, c, :], hH[:, c, :], ALU.subtract).then_inc(hl_again, 1)
            for i in range(CB):
                pool.wait_ge(cy_sig, i + 1)
                pool.tensor_tensor(cy[:, i, :], cy[:, i, :], glu[:, i, 0:T], ALU.mult).then_inc(cy_part, 1)
                pool.wait_ge(cy_part, 2 * i + 1)
                pool.tensor_copy(cyH[:, i, :], cy[:, i, :]).then_inc(cy_part, 1)
                pool.wait_ge(cy_part, 2 * i + 2)
                pool.tensor_tensor(cyL[:, i, :], cy[:, i, :], cyH[:, i, :], ALU.subtract).then_inc(cy_ready, 1)
            pool.wait_ge(hl_again, DC)
            wait_taken(pool, f"ST{2 * TT - 1}")
            pool.wait_ge(conv_out, CB - 1)
            pool.dma_start(x1[:, :, :], xT).then_inc(xr_loaded, 16)
            wait_taken(pool, f"wout{DC - 1}")
            pool.dma_start(keys[:, :, :], keysT).then_inc(s_keys, 16)

            def u_low(n, slot):
                pool.wait_ge(uh_ready, n + 1)
                pool.tensor_tensor(uL[:, slot % 2, :, :], uraw[:, slot, :, :], uH[:, slot % 2, :, :],
                                   ALU.subtract).then_inc(ul_ready, 1)

            u_low(0, 0)
            with pool.Fori(0, NPRE // 8) as i:
                for j in range(4):
                    u_low(4 * i + j + 1, (j + 1) % 4)
            for t in range(TT):
                wait_taken(pool, f"e2T{t}")
            with pool.Fori(0, NPRE // 8) as i:
                pool.tensor_copy(e2s[:, :], et[:, 1, bass.ds(2 * T_W * i, 2 * T_W)]).then_inc(pool_order, 1)
                pool.wait_ge(pool_order, i + steps + 1)
                for j in range(4):
                    for b in range(4):
                        pool.wait_ge(wmm_done, 16 * i + 4 * j + b + 1)
                        pool.sem_inc(batch_begun, 1)
                        for k in range(3):
                            tok = 16 * j + 4 * b + k
                            ins = pool.tensor_scalar(oh2[:, b, k, :], C(C_IOTA), e2s[:, tok:tok + 1], None,
                                                     ALU.is_equal)
                        ins.then_inc(oh2_ready, 1)
                pool.wait_ge(oh2_ready, 16 * i + 16)


def constants():
    i, j = np.arange(P)[:, None], np.arange(P)[None, :]
    c = np.zeros((NCONST, P, P), np.float32)
    c[C_ID] = i == j
    c[C_M1024], c[C_M512] = 1.0 / D, 1.0 / 512
    c[C_HEAD1] = i // HD == j // HD
    c[C_HEADM] = c[C_HEAD1] / HD
    same = i // CHUNK == j // CHUNK
    c[C_STRICT], c[C_INCL] = same & (i < j), same & (i <= j)
    for k, b in ((C_E1, 1), (C_E2, 2), (C_E4, 4), (C_E8, 8), (C_E16, 16), (C_E32, 32)):
        c[k] = (i // (2 * b) == j // (2 * b)) & (i % (2 * b) >= b) & (j % (2 * b) < b)
    c[C_E1T] = c[C_E1].T
    c[C_IOTA] = j + 0 * i
    reset = np.broadcast_to((np.arange(T) % CHUNK != 0).astype(np.float32), (P, T))
    return np.ascontiguousarray(c.transpose(1, 0, 2)), np.ascontiguousarray(reset)


def columns(v):
    return np.asarray(v).reshape(-1, P).T


def kernel(x, norm_mix_g, w_in, conv_dw, conv_dw_b, conv_ln_g, conv_ln_b, conv_pw, conv_pw_b,
           rw_mu, rw_w0, rw_w2, rw_a0, rw_a2, rw_g2, rw_k_k, rw_k_a, rw_r_k, rw_gn_g, rw_gn_b,
           rw_w_o, w_out, norm_ffn_g, peer_wq, peer_keys, peer_u, peer_v, norm_f_g):
    import concourse.bacc as bacc
    from concourse.bass_utils import run_bass_kernel_spmd

    def pad(v):
        return np.pad(np.asarray(v), (0, P - len(v)))[:, None]

    def blocks(w):
        w = np.asarray(w)
        return w.reshape(w.shape[0] // P, P, w.shape[1] // P, P).transpose(2, 1, 0, 3)

    w = np.asarray(w_in)[0]
    r0 = 2 * 512
    lo0, ga0 = r0 + 3 * 512, r0 + 3 * 512 + LW + LA + LG
    conv = blocks(w[:, :r0])
    order = [blocks(w[:, r0:lo0])]
    for i in range(CB):
        order += [conv[CB + i][None], conv[i][None]]
    ga, gb = blocks(w[:, ga0:ga0 + D]), blocks(w[:, ga0 + D:])
    pw, wo = blocks(conv_pw[0]), blocks(rw_w_o[0])
    for kind, d in MIX_ORDER:
        order += [(ga if kind == "a" else gb)[d][None] if kind != "p" else np.concatenate([pw[d], wo[d]], 1)[None]]
    order += [blocks(w_out[0]), blocks(peer_wq[0])]
    mu = np.asarray(rw_mu)[0]
    dw = np.asarray(conv_dw)[0].reshape(TAPS, CB, P).transpose(2, 1, 0).reshape(P, CB * TAPS)
    cols = {"gmix": columns(norm_mix_g[0]), "dw": dw, "dwb": columns(conv_dw_b[0]), "lng": columns(conv_ln_g[0]),
            "lnb": columns(conv_ln_b[0]), "pwb": columns(conv_pw_b[0]), "mu": columns(mu[:1536]),
            "mua": pad(mu[1536:1600]), "mub": pad(mu[1600:1696]), "w0": columns(rw_w0[0]), "a0": columns(rw_a0[0]),
            "kk": columns(rw_k_k[0]), "ka": columns(rw_k_a[0]), "rk": columns(np.asarray(rw_r_k)[0].reshape(-1)),
            "gng": columns(rw_gn_g[0]), "gnb": columns(rw_gn_b[0]), "gffn": columns(norm_ffn_g[0]),
            "gf": columns(norm_f_g), "eps": np.full((P, 3), (NORM_EPS, LN_EPS, GN_EPS), np.float32)}
    consts, reset = constants()
    arrays = {
        "xT": np.asarray(x)[0].T.reshape(DC, P, T).transpose(1, 0, 2),
        "consts": consts,
        "reset": reset,
        "vecs": np.concatenate([cols[n] for n, _ in VEC], 1),
        "wlora": w[:, lo0:ga0].reshape(DC, P, LW + LA + LG).transpose(1, 0, 2),
        "wall": np.concatenate(order, 0),
        "w2a2": np.concatenate([np.asarray(rw_w2)[0], np.asarray(rw_a2)[0]], 0),
        "g2": np.asarray(rw_g2)[0],
        "keysT": np.asarray(peer_keys)[0].reshape(2 * PKH, NK, P).transpose(2, 0, 1),
        "uT": np.asarray(peer_u)[0].reshape(NK, NK, DC, P).transpose(0, 3, 2, 1),
        "v_tab": np.asarray(peer_v)[0],
    }
    nc = bacc.Bacc("TRN2", target_bir_lowering=False, num_devices=1)
    args = {}
    for name, a in arrays.items():
        arrays[name] = a = np.ascontiguousarray(a)
        args[name] = nc.dram_tensor(name, a.shape, mybir.dt.from_np(a.dtype), kind="ExternalInput").ap()
    args["w_dram"] = nc.dram_tensor("w_dram", (NTB, P, NK, T_W), F32, kind="Internal").ap()
    args["g_dram"] = nc.dram_tensor("g_dram", (NPRE, P, T), F32, kind="Internal").ap()
    args["yT"] = nc.dram_tensor("yT", (DC, P, T), F32, kind="ExternalOutput").ap()
    build(nc, **args)
    r = run_bass_kernel_spmd(nc, [arrays], core_ids=[0])
    return r.results[0]["yT"].reshape(D, T).T.reshape(1, T, D)
```
